# Optimizing a Trainium2 kernel written in Bass

```python
import jax, jax.numpy as jnp
from jax import lax
import numpy as np

D_MODEL = 1024
BATCH = 1
SEQ = 256
DEPTH = 2

ATT_GROUPS = ((128, 1), (512, 4), (2048, 16))
HEADS_PER_GROUP = 4
N_ATT_HEADS = HEADS_PER_GROUP * len(ATT_GROUPS)
ATT_HEAD_DIM = 64
ATT_WIDTH = N_ATT_HEADS * ATT_HEAD_DIM
ATT_OUT_WIDTH = HEADS_PER_GROUP * ATT_HEAD_DIM
BLOCK = 128
ALIBI_MAX = 8.0
NEG_INF = -1e30
RET_HEADS = 8
RET_KEY_DIM = 64
RET_VAL_DIM = 128
RET_QK_WIDTH = RET_HEADS * RET_KEY_DIM
RET_V_WIDTH = RET_HEADS * RET_VAL_DIM
RET_CHUNK = 128
ROPE_BASE = 10000.0
D_FF = 2816
N_EXPERTS = 8
TOP_K = 2
EPS = 1e-6
IN_SIZES = (ATT_WIDTH, ATT_WIDTH, ATT_WIDTH, RET_QK_WIDTH, RET_QK_WIDTH, RET_V_WIDTH, RET_V_WIDTH, D_MODEL, D_MODEL)
IN_COLS = sum(IN_SIZES)
IN_SPLIT_POINTS = tuple(int(v) for v in np.cumsum(IN_SIZES)[:-1])

kernel_name = 'hybrid_dilated_retention_moe_block'

def rms_norm(x, gain):
    xf = x.astype(jnp.float32)
    y = xf * lax.rsqrt(jnp.mean(xf * xf, axis=-1, keepdims=True) + EPS)
    return (y * gain.astype(jnp.float32)).astype(x.dtype)

def alibi_slopes():
    h = jnp.arange(1, N_ATT_HEADS + 1, dtype=jnp.float32)
    return jnp.exp2(-ALIBI_MAX * h / N_ATT_HEADS)

def retention_gammas():
    return jnp.log1p(-jnp.exp2(-5.0 - jnp.arange(RET_HEADS, dtype=jnp.float32)))

def rotary(t, positions):
    half = t.shape[-1] // 2
    inv_freq = 1.0 / (ROPE_BASE ** (jnp.arange(half, dtype=jnp.float32) / half))
    ang = positions.astype(jnp.float32)[:, None] * inv_freq[None]
    cos = jnp.cos(ang)[None, :, None, :]
    sin = jnp.sin(ang)[None, :, None, :]
    t1, t2 = t[..., :half], t[..., half:]
    return jnp.concatenate([t1 * cos - t2 * sin, t1 * sin + t2 * cos], axis=-1)

def dilated_attention(q, k, v, window, dilation, slopes):
    B, S, H, Dh = q.shape
    n_w = window // dilation
    n = S // dilation
    nb = -(-n // BLOCK)
    pad = nb * BLOCK - n

    def to_strided(t):
        t = t.reshape(B, n, dilation, H, Dh)
        t = jnp.pad(t, ((0, 0), (0, pad), (0, 0), (0, 0), (0, 0)))
        return t.reshape(B, nb, BLOCK, dilation, H, Dh)

    def with_prev(t):
        prev = jnp.pad(t, ((0, 0), (1, 0), (0, 0), (0, 0), (0, 0), (0, 0)))[:, :-1]
        return jnp.concatenate([prev, t], axis=2)

    qs = to_strided(q)
    kb = with_prev(to_strided(k))
    vb = with_prev(to_strided(v))
    scores = jnp.einsum('bnqrhd,bnkrhd->bnrhqk', qs, kb) * (Dh ** -0.5)
    qi = jnp.arange(BLOCK)[:, None] + BLOCK
    kj = jnp.arange(2 * BLOCK)[None, :]
    dist = qi - kj
    blk = jnp.arange(nb)
    valid = ((dist >= 0) & (dist <= n_w))[None] & ((blk[:, None, None] > 0) | (kj[None] >= BLOCK))
    alibi = -slopes[:, None, None] * (dilation * dist).astype(jnp.float32)[None]
    scores = jnp.where(valid[None, :, None, None], scores + alibi, NEG_INF)
    m = jnp.max(scores, axis=-1, keepdims=True)
    p = jnp.exp(scores - m)
    den = jnp.sum(p, axis=-1, keepdims=True)
    out = jnp.einsum('bnrhqk,bnkrhd->bnqrhd', p / den, vb)
    lse = (m + jnp.log(den))[..., 0]
    out = out.reshape(B, nb * BLOCK, dilation, H, Dh)[:, :n].reshape(B, S, H, Dh)
    lse = jnp.transpose(lse, (0, 1, 4, 2, 3)).reshape(B, nb * BLOCK, dilation, H)[:, :n].reshape(B, S, H)
    return out, lse

def retention(q, k, v, log_gamma):
    B, S, H, Dk = q.shape
    Dv = v.shape[-1]
    C = RET_CHUNK
    nc = S // C
    k = k * (Dk ** -0.5)
    qc = q.reshape(B, nc, C, H, Dk)
    kc = k.reshape(B, nc, C, H, Dk)
    vc = v.reshape(B, nc, C, H, Dv)
    idx = jnp.arange(C, dtype=jnp.float32)
    rel = idx[:, None] - idx[None, :]
    decay = jnp.where(rel[None] >= 0, jnp.exp(jnp.maximum(rel, 0.0)[None] * log_gamma[:, None, None]), 0.0)
    intra = jnp.einsum('bcihd,bcjhd->bchij', qc, kc) * decay[None, None]
    intra_out = jnp.einsum('bchij,bcjhv->bcihv', intra, vc)
    zeta = jnp.exp((C - 1 - idx)[None] * log_gamma[:, None])
    xi = jnp.exp((idx + 1)[None] * log_gamma[:, None])
    chunk_kv = jnp.einsum('bcjhd,hj,bcjhv->bchdv', kc, zeta, vc)
    g_chunk = jnp.exp(C * log_gamma)[:, None, None]

    def step(state, kv):
        return state * g_chunk + kv, state

    _, r_prev = lax.scan(step, jnp.zeros((B, H, Dk, Dv), jnp.float32), jnp.moveaxis(chunk_kv, 1, 0))
    r_prev = jnp.moveaxis(r_prev, 0, 1)
    inter = jnp.einsum('bcihd,hi,bchdv->bcihv', qc, xi, r_prev)
    return (intra_out + inter).reshape(B, S, H, Dv)

def token_mixer(h, w_in, w_att_proj, w_ret_proj, w_mix_out):
    B, S, _ = h.shape
    proj = h @ w_in
    q_a, k_a, v_a, q_r, k_r, v_r, g_r, gate_a, gate_r = jnp.split(proj, IN_SPLIT_POINTS, axis=-1)
    heads = lambda t: t.astype(jnp.float32).reshape(B, S, N_ATT_HEADS, ATT_HEAD_DIM)
    q_a, k_a, v_a = heads(q_a), heads(k_a), heads(v_a)
    slopes = alibi_slopes()
    outs, lses = [], []
    for g, (window, dilation) in enumerate(ATT_GROUPS):
        sl = slice(g * HEADS_PER_GROUP, (g + 1) * HEADS_PER_GROUP)
        o, l = dilated_attention(q_a[:, :, sl], k_a[:, :, sl], v_a[:, :, sl], window, dilation, slopes[sl])
        outs.append(o)
        lses.append(l)
    weights = jax.nn.softmax(jnp.stack(lses), axis=0)
    att = jnp.sum(weights[..., None] * jnp.stack(outs), axis=0).reshape(B, S, ATT_OUT_WIDTH).astype(h.dtype)
    pos = jnp.arange(S)
    q_r = rotary(q_r.astype(jnp.float32).reshape(B, S, RET_HEADS, RET_KEY_DIM), pos)
    k_r = rotary(k_r.astype(jnp.float32).reshape(B, S, RET_HEADS, RET_KEY_DIM), pos)
    v_r = v_r.astype(jnp.float32).reshape(B, S, RET_HEADS, RET_VAL_DIM)
    ret = retention(q_r, k_r, v_r, retention_gammas())
    ret = ret * lax.rsqrt(jnp.mean(ret * ret, axis=-1, keepdims=True) + EPS)
    ret = (jax.nn.silu(g_r.astype(jnp.float32)) * ret.reshape(B, S, RET_V_WIDTH)).astype(h.dtype)
    merged = jax.nn.sigmoid(gate_a) * (att @ w_att_proj) + jax.nn.sigmoid(gate_r) * (ret @ w_ret_proj)
    return merged @ w_mix_out

def swiglu(h, w_gate, w_up, w_down):
    return (jax.nn.silu(h @ w_gate) * (h @ w_up)) @ w_down

def moe_swiglu(h, w_router, b_router, w_exp_gate, w_exp_up, w_exp_down):
    logits = (h @ w_router).astype(jnp.float32) + b_router.astype(jnp.float32)
    top_vals, top_idx = lax.top_k(logits, TOP_K)
    top_w = jax.nn.softmax(top_vals, axis=-1)
    combine = jnp.sum(jax.nn.one_hot(top_idx, N_EXPERTS, dtype=jnp.float32) * top_w[..., None], axis=-2)
    out = jnp.zeros_like(h)
    for e in range(N_EXPERTS):
        y = swiglu(h, w_exp_gate[e], w_exp_up[e], w_exp_down[e])
        out = out + combine[..., e:e + 1].astype(h.dtype) * y
    return out

def setup_inputs(seed: int = 0) -> dict:
    key = jax.random.key(seed)
    ks = jax.random.split(key, 24)
    n_dense = (DEPTH + 1) // 2
    n_moe = DEPTH // 2
    f32 = jnp.float32

    def w(k, shape, fan_in):
        return jax.random.normal(k, shape, f32) * (fan_in ** -0.5)

    def gain(k, shape):
        return 1.0 + 0.05 * jax.random.normal(k, shape, f32)

    def bias(k, shape, scale):
        return scale * jax.random.normal(k, shape, f32)

    D = D_MODEL
    return {
        'x': jax.random.normal(ks[0], (BATCH, SEQ, D), f32),
        'c': jax.random.normal(ks[1], (BATCH, D), f32),
        'w_ada': w(ks[2], (DEPTH, D, 6 * D), D),
        'b_ada': bias(ks[3], (DEPTH, 6 * D), 0.02),
        'norm_pre_mix': gain(ks[4], (DEPTH, D)),
        'w_in': w(ks[5], (DEPTH, D, IN_COLS), D),
        'w_att_proj': w(ks[6], (DEPTH, ATT_OUT_WIDTH, D), ATT_OUT_WIDTH),
        'w_ret_proj': w(ks[7], (DEPTH, RET_V_WIDTH, D), RET_V_WIDTH),
        'w_mix_out': w(ks[8], (DEPTH, D, D), D),
        'norm_post_mix': gain(ks[9], (DEPTH, D)),
        'norm_pre_ffn': gain(ks[10], (DEPTH, D)),
        'w_ffn_gate': w(ks[11], (n_dense, D, D_FF), D),
        'w_ffn_up': w(ks[12], (n_dense, D, D_FF), D),
        'w_ffn_down': w(ks[13], (n_dense, D_FF, D), D_FF),
        'w_router': w(ks[14], (n_moe, D, N_EXPERTS), D),
        'b_router': bias(ks[15], (n_moe, N_EXPERTS), 0.01),
        'w_exp_gate': w(ks[16], (n_moe, N_EXPERTS, D, D_FF), D),
        'w_exp_up': w(ks[17], (n_moe, N_EXPERTS, D, D_FF), D),
        'w_exp_down': w(ks[18], (n_moe, N_EXPERTS, D_FF, D), D_FF),
        'norm_post_ffn': gain(ks[19], (DEPTH, D)),
    }

def reference(x, c, w_ada, b_ada, norm_pre_mix, w_in, w_att_proj, w_ret_proj, w_mix_out, norm_post_mix,
              norm_pre_ffn, w_ffn_gate, w_ffn_up, w_ffn_down, w_router, b_router, w_exp_gate, w_exp_up,
              w_exp_down, norm_post_ffn):
    c_act = jax.nn.silu(c)
    for layer in range(DEPTH):
        mod = c_act @ w_ada[layer] + b_ada[layer]
        sh1, sc1, g1, sh2, sc2, g2 = jnp.split(mod[:, None, :], 6, axis=-1)
        h = rms_norm(x, norm_pre_mix[layer]) * (1.0 + sc1) + sh1
        y = token_mixer(h, w_in[layer], w_att_proj[layer], w_ret_proj[layer], w_mix_out[layer])
        x = x + g1 * rms_norm(y, norm_post_mix[layer])
        h = rms_norm(x, norm_pre_ffn[layer]) * (1.0 + sc2) + sh2
        j = layer // 2
        if layer % 2 == 0:
            y = swiglu(h, w_ffn_gate[j], w_ffn_up[j], w_ffn_down[j])
        else:
            y = moe_swiglu(h, w_router[j], b_router[j], w_exp_gate[j], w_exp_up[j], w_exp_down[j])
        x = x + g2 * rms_norm(y, norm_post_ffn[layer])
    return x


_drawn_inputs = setup_inputs


def setup_inputs(seed=0):
    import zlib

    import numpy as np

    out = dict(_drawn_inputs(seed))
    spreads = {}
    factors = {'b_router': 8.0}
    for name, (base, spread) in spreads.items():
        noise = np.random.default_rng([zlib.crc32(name.encode()), seed]).standard_normal(out[name].shape)
        drawn = base * np.exp(spread * noise) if base else spread * noise
        out[name] = __import__('jax').numpy.asarray(drawn.astype(out[name].dtype))
    for name, factor in factors.items():
        out[name] = (out[name] * factor).astype(out[name].dtype)
    return out
```

```python
from contextlib import ExitStack

import numpy as np
import concourse.bass as bass
from concourse import mybir

F32 = mybir.dt.float32
F32R = mybir.dt.float32r
I32 = mybir.dt.int32
U32 = mybir.dt.uint32
ALU = mybir.AluOpType
ACT = mybir.ActivationFunctionType
AX = mybir.AxisListType.X

P = 128
EPS = 1e-6
INVALID = 1e33

D, T, LAYERS = 1024, 256, 2
TILES = T // P
KD = D // P
HG, GROUPS, DH = 4, 3, 64
HEADS = HG * GROUPS
RH, RDK, RDV = 8, 64, 128
FF = 2816
EXPERTS = 8
GF = FF // 256
IN_COLS = 7424

QK_COLS = 2 * HEADS * DH
NAT_COLS = IN_COLS - QK_COLS
VA, QR, KR, VR, GR, GA, GB = 0, 768, 1280, 1792, 2816, 3840, 4864
WIN_GROUPS = 15
QK_GROUPS = QK_COLS // 512

SLAB = 2048
MIX_SLOTS, FFN_SLOTS, SPLIT_SLOTS = 4, 11, 3
PASS = 3 * GF


def ffn_order():
    order = [("gu", 0, 0), ("gu", 0, 1)]
    for g in range(1, GF):
        order += [("gu", g, 0), ("gu", g, 1), ("dn", g - 1, 0)]
    return order + [("dn", GF - 1, 0)]


FFN_ORDER = ffn_order()


def static_slabs():
    out = []
    for l in range(LAYERS):
        out += [("ada", l, c, q) for c in range(6) for q in range(4)]
        out += [("win", l, g, h) for g in range(WIN_GROUPS - 1) for h in range(2)] + [("win", l, WIN_GROUPS - 1, 1)]
        out += [("att", l, 0, 0)] + [("ret", l, q, 0) for q in range(4)] + [("mix", l, q, 0) for q in range(4)]
        if l == 0:
            out += [(kind, l, g, h) for kind, g, h in FFN_ORDER]
    return out


SLABS = static_slabs()
N_STATIC = len(SLABS)
FIRST = {}
for _n, _s in enumerate(SLABS):
    FIRST.setdefault(_s[:2], _n)
FFN0 = FIRST[("gu", 0)]

TR_H, TR_RQ, TR_ATT, TR_RET, TR_MIX, TR_H2 = 0, 4, 8, 9, 13, 17
TR_LAYER = 21
BACK = 4

SLOPES = [2.0 ** (-8.0 * (h + 1) / HEADS) for h in range(HEADS)]
LOG_GAMMA = [float(np.log1p(-(2.0 ** (-5.0 - h)))) for h in range(RH)]


def slab_slots():
    slot, before, use, last, count, at = [], [], [], {}, {}, 0
    for n, s in enumerate(SLABS):
        ring = FFN_SLOTS if s[0] in ("gu", "dn") else MIX_SLOTS
        if n and (s[0] in ("gu", "dn")) != (SLABS[n - 1][0] in ("gu", "dn")):
            at = 0
        j = at % ring
        at += 1
        count[j] = count.get(j, 0) + 1
        slot.append(j)
        before.append(last.get(j))
        use.append(count[j])
        last[j] = n
    return slot, before, use, last, count


SLOT, BEFORE, USE, LAST_USER, USES = slab_slots()


def host_constants():
    q = np.arange(P)[:, None]
    dist = np.full((P, GROUPS, 2, P), INVALID, np.float32)
    for g, (dil, reach) in enumerate(((1, 128), (4, 512), (16, 2048))):
        for b, shift in enumerate((P, 0)):
            d = q + shift - np.arange(P)[None]
            ok = (d >= 0) & (d <= reach) & (d % dil == 0)
            dist[:, g, b] = np.where(ok, d, INVALID)
    rel = np.full((P, 2, P), INVALID, np.float32)
    for b, shift in enumerate((0, P)):
        d = np.arange(P)[None] + shift - q
        rel[:, b] = np.where(d >= 0, d, INVALID)
    half = RDK // 2
    inv = (1.0 / (np.float32(10000.0) ** (np.arange(half, dtype=np.float32) / np.float32(half)))).astype(np.float32)
    ang = (np.arange(T, dtype=np.float32)[:, None] * inv[None]).astype(np.float32)
    trig = np.stack([np.cos(ang), np.sin(ang)], 1).astype(np.float32)
    trig = trig.reshape(TILES, P, 2 * half).transpose(1, 0, 2).reshape(P, -1)
    mix = np.concatenate([dist.reshape(P, -1), rel.reshape(P, -1), trig], 1)
    ident = np.eye(P, dtype=np.float32)
    iota = np.tile(np.arange(P, dtype=np.float32)[None], (P, 1))
    before = (np.arange(P)[:, None] < np.arange(P)[None]).astype(np.float32)
    perm = np.concatenate([ident, np.ones((P, P), np.float32), iota, before], 1)
    return np.ascontiguousarray(mix, np.float32), np.ascontiguousarray(perm, np.float32)


def hybrid_block_kernel(nc, x, c_cols, w_ada, b_ada, w_in, w_att, w_ret, w_mix, gain_cols, post_mix, post_ffn,
                        w_gate, w_up, w_down, w_router, b_router, e_gate, e_up, e_down, mix_table, perm_table, out):
    with ExitStack() as ctx:
        def sb(name, shape, dt=F32, where=ctx):
            return where.enter_context(nc.sbuf_tensor(name, shape, dt))

        def sem(name):
            return ctx.enter_context(nc.semaphore(name))

        w_hi = sb("w_hi", [P, SPLIT_SLOTS, SLAB], F32R)
        w_lo = sb("w_lo", [P, SPLIT_SLOTS, SLAB], F32R)
        raw_a = sb("raw_a", [P, MIX_SLOTS, SLAB])
        X = sb("X", [P, TILES, D])
        G = sb("G", [P, 2, D])
        xt_hi = sb("xt_hi", [P, KD, T], F32R)
        xt_lo = sb("xt_lo", [P, KD, T], F32R)
        perm = sb("perm", [P, 4, P])
        ident, ones, iota, earlier = (perm[:, i, :] for i in range(4))
        c_sb = sb("c_sb", [P, KD])
        c_act = sb("c_act", [P, KD])
        gains = sb("gains", [P, LAYERS * 2, KD])
        shift = sb("shift", [P, 2, KD])
        scale = sb("scale", [P, 2, KD])
        ssum = sb("ssum", [P, TILES])
        var = sb("var", [P, TILES])
        std = sb("std", [P, TILES])
        rstd = sb("rstd", [P, TILES])
        h_tmp = sb("h_tmp", [P, 2, T])
        router_w = sb("router_w", [P, KD, EXPERTS])
        router_b = sb("router_b", [P, EXPERTS])

        mixer = ExitStack()
        qT = sb("qT", [P, HEADS // 2, T], where=mixer)
        kT = sb("kT", [P, HEADS // 2, T], where=mixer)
        qrT = sb("qrT", [P, RH // 2, T], where=mixer)
        krT = sb("krT", [P, RH // 2, T], where=mixer)
        og = sb("og", [P, GROUPS, TILES, HG * DH], where=mixer)
        probs = sb("probs", [P, 2, 3 * P], where=mixer)
        probsT = sb("probsT", [P, 2, 3 * P], where=mixer)
        decay = sb("decay", [P, 2 * P], where=mixer)
        table = sb("table", [P, mix_table.shape[1]], where=mixer)
        dist = table[:, 0:GROUPS * 2 * P].rearrange("p (g n) -> p g n", g=GROUPS)
        rel = table[:, GROUPS * 2 * P:(GROUPS + 1) * 2 * P]
        trig = table[:, (GROUPS + 1) * 2 * P:].rearrange("p (t s n) -> p t s n", t=TILES, s=2)
        neg_max = sb("neg_max", [P, GROUPS, HG, TILES], where=mixer)
        den = sb("den", [P, GROUPS, HG, TILES], where=mixer)
        lse = sb("lse", [P, GROUPS, HG, TILES], where=mixer)
        top = sb("top", [P, HG, TILES], where=mixer)
        coef = sb("coef", [P, GROUPS, HG, TILES], where=mixer)
        r_sum = sb("r_sum", [P, TILES, RH], where=mixer)
        r_var = sb("r_var", [P, TILES, RH], where=mixer)
        r_std = sb("r_std", [P, TILES, RH], where=mixer)
        nat = sb("nat", [P, TILES, NAT_COLS], where=mixer)
        xn_mix = nat[:, 0, 0:TILES * D].rearrange("p (t d) -> p t d", t=TILES)
        mod_rows = nat[0:3, 1, 0:2 * D].rearrange("p (b d) -> p b d", b=2)
        rot = og[:, 0:2, :, :].rearrange("p g t n -> p (g t) n")
        scratch = qT[:, 0:4, :].rearrange("p c n -> p (c n)")
        mixer.close()

        h_nat = sb("h_nat", [P, TILES, D])
        y_sum = sb("y_sum", [P, TILES, D])
        act_s = sb("act_s", [P, TILES, 256])
        act_m = sb("act_m", [P, TILES, 256])
        aT_hi = sb("aT_hi", [P, TILES, 256], F32R)
        aT_lo = sb("aT_lo", [P, TILES, 256], F32R)
        xg_hi = sb("xg_hi", [P, KD, P], F32R)
        xg_lo = sb("xg_lo", [P, KD, P], F32R)
        pick = sb("pick", [P, TILES, P])
        pickT = sb("pickT", [P, T], F32R)
        logits = sb("logits", [P, TILES, EXPERTS])
        best = sb("best", [P, TILES, 8])
        best_i = sb("best_i", [P, TILES, 8], U32)
        best_f = sb("best_f", [P, TILES, 8])
        gate = sb("gate", [P, TILES, 2])
        one_hot = sb("one_hot", [P, TILES, 2, EXPERTS])
        route = sb("route", [P, TILES, 3, EXPERTS])
        route_e = sb("route_e", [P, TILES, 3])
        slot_w = sb("slot_w", [P, 1])
        counts = sb("counts", [1, EXPERTS], I32)
        raw_b = sb("raw_b", [P, FFN_SLOTS - MIX_SLOTS, SLAB])
        hT = y_sum[:, :, :].rearrange("p t (k n) -> p (t k) n", n=T)

        def raw(j):
            return raw_a[:, j, :] if j < MIX_SLOTS else raw_b[:, j - MIX_SLOTS, :]

        bank = [ctx.enter_context(nc.psum_tensor(f"ps{i}", [P, 2, 512], F32)) for i in range(4)]

        def ps(i):
            return bank[i // 2][:, i % 2, :]

        def pair(i):
            return bank[i][:, :, :].rearrange("p b n -> p (b n)")

        slab_in = [sem(f"slab_in{j}") for j in range(FFN_SLOTS)]
        hi_done, lo_done, pe_done = sem("hi_done"), sem("lo_done"), sem("pe_done")
        in_x, in_small, in_table, in_gain, in_bias = sem("in_x"), sem("in_small"), sem("in_table"), sem("in_gain"), [sem("in_bias0"), sem("in_bias1")]
        dve_step, act_step, pool_step = sem("dve_step"), sem("act_step"), sem("pool_step")
        c_ready, cs_ready = sem("c_ready"), sem("cs_ready")
        rows_ready, mod_psum, mod_done = sem("rows_ready"), sem("mod_psum"), sem("mod_done")
        ss_ready, var_ready, std_ready, xn_ready = sem("ss_ready"), sem("var_ready"), sem("std_ready"), sem("xn_ready")
        tr_psum, tr_mod, tr_hi, tr_done = sem("tr_psum"), sem("tr_mod"), sem("tr_hi"), sem("tr_done")
        ev_act, ev_dve = sem("ev_act"), sem("ev_dve")
        rot_done = sem("rot_done")
        sc_psum, sm_ready, p_ready, pT_psum, pT_ready, pv_psum, og_done = (
            sem(n) for n in ("sc_psum", "sm_ready", "p_ready", "pT_psum", "pT_ready", "pv_psum", "og_done"))
        ln_ready, lse_ready, ex_ready, att_ready = sem("ln_ready"), sem("lse_ready"), sem("ex_ready"), sem("att_ready")
        rs_psum, dec_ready, rp_ready, ro_psum, ro_done = (
            sem(n) for n in ("rs_psum", "dec_ready", "rp_ready", "ro_psum", "ro_done"))
        gates_ready, ret_ready, mrg_att, mrg_ready = sem("gates_ready"), sem("ret_ready"), sem("mrg_att"), sem("mrg_ready")
        x_done = sem("x_done")
        s_ready, a_ready, aT_psum, aT_hi_ready, aT_ready = (
            sem(n) for n in ("s_ready", "a_ready", "aT_psum", "aT_hi_ready", "aT_ready"))
        lg_psum, bd_ready, e2_ready, route_ready, rank_psum, routed = (
            sem(n) for n in ("lg_psum", "bd_ready", "e2_ready", "route_ready", "rank_psum", "routed"))
        col_ready, pick_ready, pkT_psum, pkT_ready, sw_ready = (
            sem(n) for n in ("col_ready", "pick_ready", "pkT_psum", "pkT_ready", "sw_ready"))
        xg_psum, xg_hi_ready, xg_ready = sem("xg_psum"), sem("xg_hi_ready"), sem("xg_ready")
        yh_ready, yl_ready, back_psum, y_added = sem("yh_ready"), sem("yl_ready"), sem("back_psum"), sem("y_added")
        out_sem = sem("out_sem")

        def slab_parts(kind, l, a, b, e=None):
            if kind == "ada":
                src = w_ada[l].rearrange("(k p) n -> p k n", p=P)[:, 2 * b:2 * b + 2, a * 1024:(a + 1) * 1024]
                return [(src[:, i, :], i * 1024, 1024, 1) for i in range(2)]
            if kind == "win":
                w = w_in[l].rearrange("(k p) n -> p k n", p=P)
                if a == WIN_GROUPS - 1:
                    return [(w[:, 4 * i:4 * i + 4, a * 512:IN_COLS], i * 1024, 1024, 4) for i in range(2)]
                return [(w[:, 4 * b + 2 * i:4 * b + 2 * i + 2, a * 512:(a + 1) * 512], i * 1024, 1024, 2)
                        for i in range(2)]
            if kind in ("att", "ret", "mix"):
                w = {"att": w_att, "ret": w_ret, "mix": w_mix}[kind][l].rearrange("(k p) n -> p k n", p=P)
                return [(w[:, 2 * a + i, :], i * 1024, 1024, 1) for i in range(2)]
            if kind == "gu":
                ws = (w_gate[0], w_up[0]) if e is None else (
                    e_gate[bass.ds(e, 1), :, :].rearrange("a r n -> (a r) n"),
                    e_up[bass.ds(e, 1), :, :].rearrange("a r n -> (a r) n"))
                return [(w.rearrange("(k p) n -> p k n", p=P)[:, 4 * b:4 * b + 4, a * 256:(a + 1) * 256], i, None, 4)
                        for i, w in enumerate(ws)]
            w = w_down[0] if e is None else e_down[bass.ds(e, 1), :, :].rearrange("a r n -> (a r) n")
            w = w.rearrange("(k p) n -> p k n", p=P)
            return [(w[:, 2 * a + i, :], i * 1024, 1024, 1) for i in range(2)]

        def load_slab(sp, j, parts):
            for src, at, n, chunks in parts:
                if n is None:
                    dst = raw(j).rearrange("p (k g n) -> p k g n", k=4, g=2)[:, :, at, :]
                elif chunks > 1:
                    dst = raw(j)[:, at:at + n].rearrange("p (k n) -> p k n", k=chunks)
                else:
                    dst = raw(j)[:, at:at + n]
                sp.dma_start(dst, src).then_inc(slab_in[j], 16)

        def after_pass(e, per):
            return e * per

        block = ctx.enter_context(nc.Block())

        @block.sync
        def _(sp):
            sp.dma_start(c_sb[:, :], c_cols).then_inc(in_small, 16)
            sp.dma_start(perm[:, :, :], perm_table.rearrange("p (a n) -> p a n", a=4)).then_inc(in_small, 16)
            sp.dma_start(gains[:, :, :], gain_cols.rearrange("p (a k) -> p a k", a=2 * LAYERS)).then_inc(in_small, 16)
            sp.dma_start(router_w[:, :, :], w_router[0].rearrange("(k p) e -> p k e", p=P)).then_inc(in_small, 16)
            sp.dma_start(router_b[:, :], b_router[0].partition_broadcast(P)).then_inc(in_small, 16)
            sp.dma_start(X[:, :, :], x[0].rearrange("(t p) d -> p t d", p=P)).then_inc(in_x, 16)
            for n, (kind, l, a, b) in enumerate(SLABS):
                if kind == "ada" and b == 0:
                    m = 6 * l + a
                    if a == 0 and l > 0:
                        sp.wait_ge(x_done, 2 * TILES * l)
                    if a == 0:
                        sp.dma_start(table[:, :], mix_table).then_inc(in_table, 16)
                        sp.dma_start(G[:, 0, :], post_mix[l].partition_broadcast(P)).then_inc(in_gain, 16)
                        sp.dma_start(G[:, 1, :], post_ffn[l].partition_broadcast(P)).then_inc(in_gain, 16)
                    if m >= 2:
                        sp.wait_ge(mod_psum, m - 1)
                    sp.dma_start(mod_rows[2:3, a % 2, :], b_ada[l:l + 1, a * D:(a + 1) * D]).then_inc(in_bias[a % 2], 16)
                if BEFORE[n] is not None:
                    sp.wait_ge(lo_done, BEFORE[n] + 1)
                if n == FFN0 + MIX_SLOTS:
                    sp.wait_ge(tr_psum, TR_H2)
                load_slab(sp, SLOT[n], slab_parts(kind, l, a, b))

            def expert_slabs(e, ks, nth=None):
                for k in ks:
                    if nth == 0:
                        if LAST_USER.get(k) is not None:
                            sp.wait_ge(lo_done, LAST_USER[k] + 1)
                        if k == MIX_SLOTS:
                            sp.wait_ge(tr_psum, TR_LAYER + TR_H2)
                    else:
                        sp.wait_ge(lo_done, e * PASS + (N_STATIC + k - FFN_SLOTS + 1))
                    load_slab(sp, k % FFN_SLOTS, slab_parts(*((FFN_ORDER[k][0], 1) + FFN_ORDER[k][1:]), e=e))

            expert_slabs(0, range(FFN_SLOTS), nth=0)
            with sp.Fori(0, EXPERTS - 1) as e:
                expert_slabs(e, range(FFN_SLOTS, PASS))
                e1 = sp.snap(e + 1)
                expert_slabs(e1, range(FFN_SLOTS))
            expert_slabs(EXPERTS - 1, range(FFN_SLOTS, PASS))
            for t in range(TILES):
                sp.wait_ge(x_done, 2 * TILES * LAYERS - TILES + t + 1)
                sp.dma_start(out[0].rearrange("(t p) d -> p t d", p=P)[:, t, :], X[:, t, :]).then_inc(out_sem, 16)
            sp.wait_ge(out_sem, 16 * TILES)

        @block.gpsimd
        def _(pool):
            steps = [0]

            def link(ins):
                steps[0] += 1
                ins.then_inc(pool_step, 1)
                pool.wait_ge(pool_step, steps[0])

            for l in range(LAYERS):
                pool.wait_ge(in_table, 16 * (l + 1))
                pool.wait_ge(ev_act, WIN_GROUPS * l + 7)
                pool.wait_ge(ev_dve, WIN_GROUPS * l + 7)
                for t in range(TILES):
                    cos, sin = (trig[:, t, s:s + 1, :].to_broadcast([P, RH, 32]) for s in range(2))
                    for at in (QR, KR):
                        v = nat[:, t, at:at + 512].rearrange("p (h s n) -> p h s n", h=RH, s=2)
                        r = [rot[:, i, :].rearrange("p (h n) -> p h n", h=RH) for i in range(4)]
                        pool.tensor_tensor(r[0], v[:, :, 0, :], cos, ALU.mult)
                        pool.tensor_tensor(r[1], v[:, :, 1, :], sin, ALU.mult)
                        pool.tensor_tensor(r[2], v[:, :, 0, :], sin, ALU.mult)
                        link(pool.tensor_tensor(r[3], v[:, :, 1, :], cos, ALU.mult))
                        pool.tensor_tensor(v[:, :, 0, :], r[0], r[1], ALU.subtract)
                        ins = pool.tensor_tensor(v[:, :, 1, :], r[2], r[3], ALU.add)
                        if (t, at) == (TILES - 1, KR):
                            ins.then_inc(rot_done, 1)
                        else:
                            link(ins)

        @block.scalar
        def _(act):
            def split_hi(n, at, value):
                act.activation(w_hi[:, at % SPLIT_SLOTS, :], raw(value), ACT.Copy).then_inc(hi_done, 1)

            def static_split(n):
                act.wait_ge(slab_in[SLOT[n]], 32 * USE[n])
                if n >= SPLIT_SLOTS:
                    act.wait_ge(pe_done, n - SPLIT_SLOTS + 1)
                split_hi(n, n, SLOT[n])

            def tr_high(step, dst, src=None):
                if src is None:
                    act.wait_ge(tr_psum, step + 1)
                    src = ps(6 + step % 2)
                act.activation(dst, src, ACT.Copy).then_inc(tr_hi, 1)

            def sum_squares(srcs):
                for t, src in enumerate(srcs):
                    junk = xt_hi[:, 4 * t:4 * t + 4, :].rearrange("p k n -> p (k n)")
                    act.activation(junk, src, ACT.Square, accum_out=ssum[:, t:t + 1]).then_inc(ss_ready, 1)

            def root(k):
                act.wait_ge(var_ready, k + 1)
                act.activation(std[:, :], var[:, :], ACT.Sqrt).then_inc(std_ready, 1)

            def group_silu(tiles, e, g, slab_end, first):
                act.wait_ge(pe_done, slab_end)
                if first is not None:
                    act.wait_ge(a_ready, first)
                v = bank[g % 2][:, 0:tiles, 0:256]
                act.activation(act_s[:, 0:tiles, :], v, ACT.Silu).then_inc(s_ready, 1)

            def group_aT(tiles, g, count):
                act.wait_ge(aT_psum, count)
                v = bank[g % 2][:, 0:tiles, 0:256]
                act.activation(aT_hi[:, 0:tiles, :], v, ACT.Copy).then_inc(aT_hi_ready, 1)

            def ffn_task(k, tiles, slab0, group0):
                kind, g, h = FFN_ORDER[k]
                if (kind, h) == ("gu", 1):
                    group_silu(tiles, None, g, slab0 + (k + 1), None if isinstance(group0, int) and group0 + g == 0 else group0 + g)
                if ((kind, h) == ("gu", 0) and g > 0) or (kind, g) == ("dn", GF - 2):
                    q = g - 1 if kind == "gu" else GF - 1
                    group_aT(tiles, q, group0 + (q + 1))

            act.wait_ge(in_small, 16 * 5)
            act.activation(c_act[:, :], c_sb[:, :], ACT.Silu).then_inc(c_ready, 1)
            norm = 0
            for l in range(LAYERS):
                tr = TR_LAYER * l
                n0 = FIRST[("ada", l)]
                if l:
                    act.wait_ge(x_done, 2 * TILES * l)
                else:
                    act.wait_ge(c_ready, 1)
                act.wait_ge(cs_ready, 2 * l + 1)
                act.activation(xt_hi[:, :, 0], c_act[:, :], ACT.Copy).then_inc(cs_ready, 1)

                def rows_out(n):
                    if SLABS[n][0] == "ada" and SLABS[n][3] == 3:
                        a = SLABS[n][2]
                        m = 6 * l + a
                        act.wait_ge(pe_done, n + 1)
                        if m >= 2:
                            act.wait_ge(mod_psum, m - 1)
                        act.activation(mod_rows[0:2, a % 2, :], pair(a % 2)[0:2, :], ACT.Copy).then_inc(rows_ready, 1)

                for n in range(n0, n0 + 24):
                    static_split(n)
                    if n > n0:
                        rows_out(n - 1)
                rows_out(n0 + 23)
                if l == 0:
                    act.wait_ge(in_x, 16)
                act.wait_ge(pe_done, n0 + 24)
                sum_squares([X[:, t, :] for t in range(TILES)])
                root(norm); norm += 1
                for s in range(4):
                    act.wait_ge(tr_mod, 4 * 2 * l + s + 1)
                    tr_high(tr + TR_H + s, xt_hi[:, 2 * s:2 * s + 2, :], h_tmp[:, :, :])
                n0 = FIRST[("win", l)]

                def win_out(n):
                    _, _, g, h = SLABS[n]
                    if h == 0:
                        return
                    act.wait_ge(pe_done, n + 1)
                    src = bank[g % 2][:, 0, :]
                    if g < QK_GROUPS:
                        dst, at = (qT, 4 * g) if 4 * g < 6 else (kT, 4 * g - 6)
                        dst = dst[:, at:at + 2, :].rearrange("p c n -> p (c n)")
                        act.activation(dst, src, ACT.Copy, scale=(0.125 if 4 * g < 6 else 1.0)).then_inc(ev_act, 1)
                    else:
                        w = min(512, NAT_COLS - (g - QK_GROUPS) * 512)
                        at = (g - QK_GROUPS) * 512
                        act.activation(nat[:, 0, at:at + w], src[:, 0:w], ACT.Copy).then_inc(ev_act, 1)

                for n in range(n0, n0 + 29):
                    static_split(n)
                    if n > n0:
                        win_out(n - 1)
                win_out(n0 + 28)
                for i in range(HEADS + 1):
                    h = HEADS * l + i
                    if i < HEADS:
                        g, hh = divmod(i, HG)
                        act.wait_ge(sm_ready, h + 1)
                        for t in range(TILES):
                            v = probs[:, i % 2, 0:P] if t == 0 else probs[:, i % 2, P:3 * P]
                            ins = act.activation(v, v, ACT.Exp, bias=neg_max[:, g, hh, t:t + 1],
                                                 accum_out=den[:, g, hh, t:t + 1])
                            ins.then_inc(p_ready, 1)
                    if i >= 1:
                        act.wait_ge(pT_psum, h)
                        if h >= 3:
                            act.wait_ge(pv_psum, h - 2)
                        act.activation(probsT[:, (i - 1) % 2, :], ps((i - 1) % 2)[:, 0:3 * P], ACT.Copy).then_inc(pT_ready, 1)
                act.wait_ge(p_ready, 2 * HEADS * (l + 1))
                act.activation(lse[:, :, :, :], den[:, :, :, :], ACT.Ln).then_inc(ln_ready, 1)
                act.wait_ge(lse_ready, l + 1)
                act.activation(coef[:, :, :, :], lse[:, :, :, :], ACT.Exp).then_inc(ex_ready, 1)
                act.wait_ge(in_table, 16 * (l + 1))
                for r in range(RH):
                    k = RH * l + r
                    if k:
                        act.wait_ge(rp_ready, k)
                    act.activation(decay[:, :], rel, ACT.Exp, scale=LOG_GAMMA[r]).then_inc(dec_ready, 1)
                act.wait_ge(ev_dve, WIN_GROUPS * (l + 1))
                act.wait_ge(ev_act, WIN_GROUPS * (l + 1))
                for t in range(TILES):
                    v = nat[:, t, GA:GA + 2 * D]
                    act.activation(v, v, ACT.Sigmoid).then_inc(gates_ready, 1)
                for t in range(TILES):
                    v = nat[:, t, GR:GR + D]
                    act.activation(v, v, ACT.Silu).then_inc(gates_ready, 1)
                act.wait_ge(var_ready, norm + 1)
                act.activation(r_std[:, :, :], r_var[:, :, :], ACT.Sqrt).then_inc(std_ready, 1)
                norm += 1
                tr_high(tr + TR_ATT, xt_hi[:, 0:2, :])
                n = FIRST[("att", l)]
                static_split(n)
                for s in range(4):
                    tr_high(tr + TR_RET + s, xt_hi[:, 2 * s:2 * s + 2, :])
                for q in range(4):
                    static_split(n + 1 + q)
                for s in range(4):
                    tr_high(tr + TR_MIX + s, xt_hi[:, 2 * s:2 * s + 2, :])
                for q in range(4):
                    static_split(n + 5 + q)
                act.wait_ge(pe_done, n + 9)
                sum_squares([pair(t) for t in range(TILES)])
                root(norm); norm += 1
                act.wait_ge(x_done, 2 * TILES * l + TILES)
                sum_squares([X[:, t, :] for t in range(TILES)])
                root(norm); norm += 1
                for s in range(4):
                    act.wait_ge(tr_mod, 4 * (2 * l + 1) + s + 1)
                    src = h_tmp[:, :, :] if l == 0 else hT[:, 2 * s:2 * s + 2, :]
                    tr_high(tr + TR_H2 + s, xt_hi[:, 2 * s:2 * s + 2, :], src)
                if l == 0:
                    for k in range(PASS):
                        static_split(FFN0 + k)
                        if k:
                            ffn_task(k - 1, TILES, FFN0, 0)
                    act.wait_ge(pe_done, FFN0 + PASS)
                    sum_squares([pair(2 + t) for t in range(TILES)])
                    root(norm); norm += 1

            act.wait_ge(bd_ready, 1)
            act.activation(gate[:, :, 1], gate[:, :, 0], ACT.Exp).then_inc(e2_ready, 1)
            act.wait_ge(routed, 1)

            with act.Fori(0, EXPERTS) as e:
                slab0 = act.snap(e * PASS + N_STATIC)
                group0 = act.snap(e * GF + GF)
                uses = act.snap(e * 96)
                count = act.value_load(counts[0:1, bass.ds(e, 1)], min_val=0, max_val=T)
                act.wait_ge(pkT_psum, e + 1)
                act.activation(pickT[:, :], ps(7)[:, 0:T], ACT.Copy).then_inc(pkT_ready, 1)
                for s in range(2):
                    act.wait_ge(xg_psum, e * 2 + (s + 1))
                    dst = xg_hi[:, 4 * s:4 * s + 4, :].rearrange("p k n -> p (k n)")
                    act.activation(dst, ps(6 + s), ACT.Copy).then_inc(xg_hi_ready, 1)

                def expert(tiles):
                    for k in range(PASS):
                        j = k % FFN_SLOTS
                        act.wait_ge(slab_in[j], uses + 32 * (USES.get(j, 0) + k // FFN_SLOTS + 1))
                        act.wait_ge(pe_done, slab0 + (k - SPLIT_SLOTS + 1))
                        split_hi(None, N_STATIC + k, j)
                        if k:
                            ffn_task(k - 1, tiles, slab0, group0)

                with act.If(count > P):
                    expert(TILES)
                    act.sem_inc(yh_ready, 1)
                with act.Else():
                    expert(1)
                    act.wait_ge(pe_done, slab0 + PASS)
                    act.wait_ge(sw_ready, e + 1)
                    act.activation(xg_hi[:, :, :].rearrange("p k n -> p (k n)"), pair(2), ACT.Copy,
                                   scale=slot_w[:, 0:1]).then_inc(yh_ready, 1)

            act.wait_ge(y_added, 4 * (EXPERTS + 1))
            sum_squares([y_sum[:, t, :] for t in range(TILES)])
            root(norm)

        @block.tensor
        def _(pe):
            def product(outs, xs, n_at, col, width, first, last):
                whi = w_hi[:, n_at % SPLIT_SLOTS, col:col + width]
                wlo = w_lo[:, n_at % SPLIT_SLOTS, col:col + width]
                for o, (xh, xl) in zip(outs, xs):
                    pe.matmul(o, xh, whi, start=first, stop=False)
                    pe.matmul(o, xh, wlo, start=False, stop=False)
                    ins = pe.matmul(o, xl, whi, start=False, stop=last)
                return ins

            def xt(t, k):
                return xt_hi[:, k, t * P:(t + 1) * P], xt_lo[:, k, t * P:(t + 1) * P]

            def rows_slab(n, q, kinds, banks):
                pe.wait_ge(lo_done, n + 1)
                total = kinds
                for i in range(2):
                    k = 2 * q + i
                    for half in range(2):
                        outs = [ps(banks + 2 * t + half) for t in range(TILES)]
                        ins = product(outs, [xt(t, k) for t in range(TILES)], n, i * 1024 + half * 512, 512,
                                      k == 0, k == total - 1)
                ins.then_inc(pe_done, 1)

            def turn(step, blocks):
                if step >= 2:
                    pe.wait_ge(tr_done, step - 1)
                for i, src in enumerate(blocks):
                    ins = pe.transpose(ps(6 + step % 2)[:, i * P:(i + 1) * P], src, ident)
                ins.then_inc(tr_psum, 1)

            def turn_all(step0, src):
                for s in range(4):
                    turn(step0 + s, [src(t, 2 * s + kk) for kk in range(2) for t in range(TILES)])

            def ffn(tiles, order0, slab_value, group_value, x_of, banks_free):
                for k, (kind, g, h) in enumerate(FFN_ORDER):
                    n_at = order0 + k
                    if kind == "gu" and h == 0 and g >= 2:
                        pe.wait_ge(aT_ready, group_value + (g - 1))
                    if kind == "gu":
                        if k == 0:
                            banks_free()
                        pe.wait_ge(lo_done, slab_value + (k + 1))
                        for kk in range(4):
                            kc = 4 * h + kk
                            ins = product([ps(2 * (g % 2) + t) for t in range(tiles)],
                                          [x_of(t, kc) for t in range(tiles)], n_at, kk * 512, 512, kc == 0, kc == KD - 1)
                        ins.then_inc(pe_done, 1)
                    else:
                        pe.wait_ge(lo_done, slab_value + (k + 1))
                        pe.wait_ge(aT_ready, group_value + (g + 1))
                        for i in range(2):
                            xs = [(aT_hi[:, t, i * P:(i + 1) * P], aT_lo[:, t, i * P:(i + 1) * P]) for t in range(tiles)]
                            for half in range(2):
                                ins = product([ps(4 + 2 * t + half) for t in range(tiles)], xs, n_at,
                                              i * 1024 + half * 512, 512, g == 0 and i == 0, g == GF - 1 and i == 1)
                        ins.then_inc(pe_done, 1)
                    if (kind == "gu" and h == 0 and g > 0) or (kind == "dn" and g == GF - 2):
                        q = g - 1 if kind == "gu" else GF - 1
                        pe.wait_ge(a_ready, group_value + (q + 1))
                        for t in range(tiles):
                            for i in range(2):
                                ins = pe.transpose(ps(2 * (q % 2) + t)[:, i * P:(i + 1) * P],
                                                   act_m[:, t, i * P:(i + 1) * P], ident)
                        ins.then_inc(aT_psum, 1)

            pe.wait_ge(in_small, 16 * 5)
            for l in range(LAYERS):
                tr = TR_LAYER * l
                n0 = FIRST[("ada", l)]
                pe.wait_ge(cs_ready, 2 * l + 2)
                pe.wait_ge(tr_mod, 8 * l) if l else None

                def mod_out(a):
                    m = 6 * l + a
                    pe.wait_ge(rows_ready, m + 1)
                    pe.wait_ge(in_bias[a % 2], 16 * (3 * l + a // 2 + 1))
                    if m:
                        pe.wait_ge(mod_done, m)
                    if a % 3 == 2:
                        for half in range(2):
                            ins = pe.matmul(ps(4 + half), ones[0:3, :], mod_rows[:, a % 2, half * 512:(half + 1) * 512],
                                            start=True, stop=True)
                    else:
                        for k in range(KD):
                            ins = pe.matmul(ps(4)[:, k:k + 1], mod_rows[:, a % 2, k * P:(k + 1) * P], ones[0:3, 0:1],
                                            start=True, stop=True)
                    ins.then_inc(mod_psum, 1)

                pe.wait_ge(cs_ready, 2 * l + 2)
                pe.wait_ge(c_ready, 2 + l)
                for a in range(6):
                    for q in range(4):
                        n = n0 + 4 * a + q
                        pe.wait_ge(lo_done, n + 1)
                        if q == 0 and a >= 2:
                            pe.wait_ge(rows_ready, 6 * l + a - 1)
                        for i in range(2):
                            k = 2 * q + i
                            for half in range(2):
                                o = ps(2 * (a % 2) + half)[0:66, :]
                                col = i * 1024 + half * 512
                                pe.matmul(o, xt_hi[:, k, 0:66], w_hi[:, n % SPLIT_SLOTS, col:col + 512],
                                          start=(k == 0), stop=False)
                                ins = pe.matmul(o, xt_lo[:, k, 0:66], w_lo[:, n % SPLIT_SLOTS, col:col + 512],
                                                start=False, stop=(k == KD - 1))
                        ins.then_inc(pe_done, 1)
                        if q == 0 and a:
                            mod_out(a - 1)
                mod_out(5)
                pe.wait_ge(xn_ready, 2 * TILES * l + TILES)
                turn_all(tr + TR_H, lambda t, k: xn_mix[:, t, k * P:(k + 1) * P])
                n0 = FIRST[("win", l)]
                pe.wait_ge(tr_done, tr + TR_H + 4)
                pe.wait_ge(rows_ready, 6 * l + 6)
                for n in range(n0, n0 + 29):
                    _, _, g, h = SLABS[n]
                    s = g % 2
                    if g >= 2 and (h == 0 or g == WIN_GROUPS - 1):
                        pe.wait_ge(ev_act, WIN_GROUPS * l + g - 1)
                        pe.wait_ge(ev_dve, WIN_GROUPS * l + g - 1)
                    pe.wait_ge(lo_done, n + 1)
                    at = n % SPLIT_SLOTS
                    if g < QK_GROUPS:
                        for kk in range(4):
                            k = 4 * h + kk
                            for b in range(4):
                                o = bank[s][:, b // 2, (b % 2) * T:(b % 2 + 1) * T]
                                wh = w_hi[:, at, kk * 512 + b * P:kk * 512 + (b + 1) * P]
                                wl = w_lo[:, at, kk * 512 + b * P:kk * 512 + (b + 1) * P]
                                pe.matmul(o, wh, xt_hi[:, k, :], start=(k == 0 and b % 2 == 0), stop=False,
                                          skip_group_check=True)
                                pe.matmul(o, wh, xt_lo[:, k, :], start=False, stop=False, skip_group_check=True)
                                ins = pe.matmul(o, wl, xt_hi[:, k, :], start=False, stop=(k == KD - 1),
                                                skip_group_check=True)
                    elif g < WIN_GROUPS - 1:
                        for kk in range(4):
                            k = 4 * h + kk
                            ins = product([ps(2 * s + t) for t in range(TILES)], [xt(t, k) for t in range(TILES)], n,
                                          kk * 512, 512, k == 0, k == KD - 1)
                    else:
                        for k in range(KD):
                            ins = product([ps(2 * s + t)[:, 0:256] for t in range(TILES)],
                                          [xt(t, k) for t in range(TILES)], n, k * 256, 256, k == 0, k == KD - 1)
                    ins.then_inc(pe_done, 1)
                pe.wait_ge(ev_act, WIN_GROUPS * (l + 1))
                pe.wait_ge(ev_dve, WIN_GROUPS * (l + 1))
                for i in range(HEADS + 2):
                    if i < HEADS:
                        h = HEADS * l + i
                        pr = slice(64 * (i % 2), 64 * (i % 2) + 64)
                        if h >= 2:
                            pe.wait_ge(sm_ready, h - 1)
                        o = ps(4 + i % 2)
                        pe.matmul(o[:, 0:P], qT[pr, i // 2, 0:P], kT[pr, i // 2, 0:P], start=True, stop=True)
                        pe.matmul(o[:, P:3 * P], qT[pr, i // 2, P:T], kT[pr, i // 2, :], start=True, stop=True)\
                          .then_inc(sc_psum, 1)
                    if 1 <= i <= HEADS:
                        j = i - 1
                        h = HEADS * l + j
                        pe.wait_ge(p_ready, 2 * h + 2)
                        if h >= 2:
                            pe.wait_ge(pT_ready, h - 1)
                        for b in range(3):
                            ins = pe.transpose(ps(j % 2)[:, b * P:(b + 1) * P], probs[:, j % 2, b * P:(b + 1) * P], ident)
                        ins.then_inc(pT_psum, 1)
                    if i >= 2:
                        j = i - 2
                        h = HEADS * l + j
                        g, hh = divmod(j, HG)
                        pe.wait_ge(pT_ready, h + 1)
                        if hh == 0 and g == 2:
                            pe.wait_ge(og_done, GROUPS * l + 1)
                        o = ps(2 + g % 2).rearrange("p (t n) -> p t n", t=TILES)
                        v = [nat[:, t, VA + j * DH:VA + (j + 1) * DH] for t in range(TILES)]
                        w = probsT[:, j % 2, :]
                        pe.matmul(o[:, 0, hh * DH:(hh + 1) * DH], w[:, 0:P], v[0], start=True, stop=True)
                        pe.matmul(o[:, 1, hh * DH:(hh + 1) * DH], w[:, P:2 * P], v[0], start=True, stop=False)
                        pe.matmul(o[:, 1, hh * DH:(hh + 1) * DH], w[:, 2 * P:3 * P], v[1], start=False, stop=True)\
                          .then_inc(pv_psum, 1)
                pe.wait_ge(rot_done, l + 1)
                for s in range(4):
                    at = (QR, KR)[s // 2]
                    blocks = [nat[:, t, at + (2 * (s % 2) + kk) * P:at + (2 * (s % 2) + kk + 1) * P]
                              for kk in range(2) for t in range(TILES)]
                    turn(tr + TR_RQ + s, blocks)
                pe.wait_ge(tr_done, tr + TR_RQ + 4)
                pe.wait_ge(sm_ready, HEADS * (l + 1))
                pe.wait_ge(og_done, GROUPS * (l + 1))
                for i in range(RH + 1):
                    if i < RH:
                        r = RH * l + i
                        pr = slice(64 * (i % 2), 64 * (i % 2) + 64)
                        if r >= 2:
                            pe.wait_ge(rp_ready, r - 1)
                        o = ps(4 + i % 2)
                        pe.matmul(o[:, 0:T], krT[pr, i // 2, 0:P], qrT[pr, i // 2, :], start=True, stop=True)
                        pe.matmul(o[:, T:T + P], krT[pr, i // 2, P:T], qrT[pr, i // 2, P:T], start=True, stop=True)\
                          .then_inc(rs_psum, 1)
                    if i >= 1:
                        j = i - 1
                        r = RH * l + j
                        pe.wait_ge(rp_ready, r + 1)
                        if r >= 2:
                            pe.wait_ge(ro_done, r - 1)
                        o = ps(2 + j % 2)
                        v = [nat[:, t, VR + j * RDV:VR + (j + 1) * RDV] for t in range(TILES)]
                        w = probs[:, j % 2, :]
                        pe.matmul(o[:, 0:P], w[:, 0:P], v[0], start=True, stop=True)
                        pe.matmul(o[:, P:2 * P], w[:, P:2 * P], v[0], start=True, stop=False)
                        pe.matmul(o[:, P:2 * P], w[:, 2 * P:3 * P], v[1], start=False, stop=True).then_inc(ro_psum, 1)
                n = FIRST[("att", l)]
                pe.wait_ge(att_ready, l + 1)
                turn(tr + TR_ATT, [og[:, 0, t, kk * P:(kk + 1) * P] for kk in range(2) for t in range(TILES)])
                pe.wait_ge(tr_done, tr + TR_ATT + 1)
                pe.wait_ge(ro_done, RH * (l + 1))
                rows_slab(n, 0, 2, 0)
                pe.wait_ge(ret_ready, l + 1)
                turn_all(tr + TR_RET, lambda t, k: nat[:, t, QR + k * P:QR + (k + 1) * P])
                pe.wait_ge(tr_done, tr + TR_RET + 4)
                pe.wait_ge(mrg_att, l + 1)
                for q in range(4):
                    rows_slab(n + 1 + q, q, KD, 0)
                pe.wait_ge(mrg_ready, l + 1)
                turn_all(tr + TR_MIX, lambda t, k: nat[:, t, GA + k * P:GA + (k + 1) * P])
                pe.wait_ge(tr_done, tr + TR_MIX + 4)
                for q in range(4):
                    rows_slab(n + 5 + q, q, KD, 0)
                pe.wait_ge(xn_ready, 2 * TILES * l + 2 * TILES)
                turn_all(tr + TR_H2, lambda t, k: h_nat[:, t, k * P:(k + 1) * P])
                pe.wait_ge(tr_done, tr + TR_H2 + 4)
                if l == 0:
                    ffn(TILES, FFN0, FFN0, 0, xt, lambda: None)

            for s in range(4):
                turn(2 * TR_LAYER + s, [hT[:, 2 * s + kk, t * P:(t + 1) * P] for kk in range(2) for t in range(TILES)])
            for t in range(TILES):
                for k in range(KD):
                    ins = pe.matmul(ps(4 + t)[:, 0:EXPERTS], hT[:, k, t * P:(t + 1) * P], router_w[:, k, :],
                                    start=(k == 0), stop=(k == KD - 1))
                ins.then_inc(lg_psum, 1)
            pe.wait_ge(route_ready, 1)
            member = [route[:, t, 0, :] for t in range(TILES)]
            pe.matmul(ps(0)[:, 0:EXPERTS], earlier, member[0], start=True, stop=True)
            pe.matmul(ps(1)[:, 0:EXPERTS], ones, member[0], start=True, stop=False)
            pe.matmul(ps(1)[:, 0:EXPERTS], earlier, member[1], start=False, stop=True)
            pe.matmul(ps(2)[0:1, 0:EXPERTS], ones[:, 0:1], member[0], start=True, stop=False)
            pe.matmul(ps(2)[0:1, 0:EXPERTS], ones[:, 0:1], member[1], start=False, stop=True).then_inc(rank_psum, 1)
            pe.wait_ge(routed, 1)

            with pe.Fori(0, EXPERTS) as e:
                slab0 = pe.snap(e * PASS + N_STATIC)
                group0 = pe.snap(e * GF + GF)
                count = pe.value_load(counts[0:1, bass.ds(e, 1)], min_val=0, max_val=T)
                pe.wait_ge(y_added, e * 4 + 4)
                pe.wait_ge(pick_ready, e * 2 + 2)
                for t in range(TILES):
                    pe.transpose(ps(7)[:, t * P:(t + 1) * P], pick[:, t, :], ident)
                for t in range(TILES):
                    ins = pe.matmul(ps(7)[:, T:T + 1], pick[:, t, :], route_e[:, t, 2:3], start=(t == 0), stop=(t == 1))
                ins.then_inc(pkT_psum, 1)
                for s in range(2):
                    if s == 1:
                        pe.wait_ge(pkT_ready, e + 1)
                        pe.wait_ge(sw_ready, e + 1)
                    for kk in range(4):
                        k = 4 * s + kk
                        for t in range(TILES):
                            ins = pe.matmul(ps(6 + s)[:, kk * P:(kk + 1) * P], h_nat[:, t, k * P:(k + 1) * P],
                                            pick[:, t, :], start=(t == 0), stop=(t == 1))
                    ins.then_inc(xg_psum, 1)
                pe.wait_ge(xg_ready, e * 2 + 2)
                with pe.If(count > P):
                    ffn(TILES, N_STATIC, slab0, group0, xt, lambda: None)
                    pe.sem_inc(back_psum, 4)
                with pe.Else():
                    ffn(1, N_STATIC, slab0, group0, lambda t, k: (xg_hi[:, k, :], xg_lo[:, k, :]), lambda: None)
                    pe.wait_ge(yl_ready, e + 1)
                    for i in range(4):
                        t, half = divmod(i, 2)
                        if i >= 2:
                            pe.wait_ge(y_added, e * 4 + (4 + i - 1))
                        o = ps(6 + i % 2)
                        for j, part in enumerate((xg_hi, xg_lo)):
                            y = part[:, 4 * half:4 * half + 4, :].rearrange("p k n -> p (k n)")
                            ins = pe.matmul(o, pickT[:, t * P:(t + 1) * P], y, start=(j == 0), stop=(j == 1))
                        ins.then_inc(back_psum, 1)

        @block.vector
        def _(dve):
            steps = [0]

            def link(ins):
                steps[0] += 1
                ins.then_inc(dve_step, 1)
                dve.wait_ge(dve_step, steps[0])

            def split_lo(at, j):
                a = at % SPLIT_SLOTS
                dve.tensor_tensor(w_lo[:, a, :], raw(j), w_hi[:, a, :].bitcast(F32), ALU.subtract).then_inc(lo_done, 1)

            def static_split(n):
                dve.wait_ge(hi_done, n + 1)
                split_lo(n, SLOT[n])

            def tr_low(step, hi, lo, src=None):
                dve.wait_ge(tr_hi, step_hi[0] + 1)
                step_hi[0] += 1
                dve.tensor_tensor(lo, ps(6 + step % 2) if src is None else src, hi.bitcast(F32), ALU.subtract)\
                   .then_inc(tr_done, 1)

            step_hi = [0]

            def variance(k, n):
                dve.wait_ge(ss_ready, TILES * (k_ss[0] + 1))
                k_ss[0] += 1
                dve.tensor_scalar(var[:, :], ssum[:, :], 1.0 / n, EPS, ALU.mult, ALU.add).then_inc(var_ready, 1)
                dve.wait_ge(std_ready, k + 1)
                link(dve.reciprocal(rstd[:, :], std[:, :]))

            k_ss = [0]

            def modulated(l, which, step0, keep):
                m0 = 4 * (2 * l + which)
                for s in range(4):
                    step = step0 + s
                    dve.wait_ge(tr_psum, step + 1)
                    if keep is None and s:
                        dve.wait_ge(tr_done, step)
                    dst = h_tmp[:, :, :] if keep is None else keep[:, 2 * s:2 * s + 2, :]
                    for i in range(2):
                        k = 2 * s + i
                        ins = dve.tensor_scalar(dst[:, i, :], ps(6 + step % 2)[:, i * T:(i + 1) * T],
                                                scale[:, which, k:k + 1], shift[:, which, k:k + 1], ALU.mult, ALU.add)
                        ins.then_inc(tr_mod, i)if i else link(ins)
                    tr_low(step, xt_hi[:, 2 * s:2 * s + 2, :], xt_lo[:, 2 * s:2 * s + 2, :], dst)

            def plain(step0, steps_n):
                for s in range(steps_n):
                    src = ps(6 + (step0 + s) % 2).rearrange("p (c n) -> p c n", c=2)
                    tr_low(step0 + s, xt_hi[:, 2 * s:2 * s + 2, :], xt_lo[:, 2 * s:2 * s + 2, :], src)

            def add_norm(l, which, srcs, tmp):
                for t in range(TILES):
                    if t:
                        dve.wait_ge(x_done, 2 * TILES * l + TILES * which + t)
                    link(dve.scalar_tensor_tensor(tmp, srcs[t], rstd[:, t:t + 1], G[:, which, :], ALU.mult, ALU.mult))
                    dve.tensor_tensor(X[:, t, :], X[:, t, :], tmp, ALU.add).then_inc(x_done, 1)
                dve.wait_ge(x_done, 2 * TILES * l + TILES * (which + 1))

            def normed(dst):
                for t in range(TILES):
                    dve.tensor_scalar(dst[:, t, :], X[:, t, :], rstd[:, t:t + 1], None, ALU.mult).then_inc(xn_ready, 1)

            def group_mul(tiles, g, s_value, aT_value):
                dve.wait_ge(s_ready, s_value)
                if aT_value is not None:
                    dve.wait_ge(aT_psum, aT_value)
                v = bank[g % 2][:, 0:tiles, 256:512]
                dve.tensor_tensor(act_m[:, 0:tiles, :], act_s[:, 0:tiles, :], v, ALU.mult).then_inc(a_ready, 1)

            def group_low(tiles, g, value):
                dve.wait_ge(aT_hi_ready, value)
                v = bank[g % 2][:, 0:tiles, 0:256]
                dve.tensor_tensor(aT_lo[:, 0:tiles, :], v, aT_hi[:, 0:tiles, :].bitcast(F32), ALU.subtract)\
                   .then_inc(aT_ready, 1)

            def ffn_task(k, tiles, group0):
                kind, g, h = FFN_ORDER[k]
                if (kind, h) == ("gu", 1):
                    first = isinstance(group0, int) and group0 + g == 0
                    group_mul(tiles, g, group0 + (g + 1), None if first else group0 + g)
                if ((kind, h) == ("gu", 0) and g > 0) or (kind, g) == ("dn", GF - 2):
                    q = g - 1 if kind == "gu" else GF - 1
                    group_low(tiles, q, group0 + (q + 1))

            dve.wait_ge(c_ready, 1)
            norm = 0
            for l in range(LAYERS):
                tr = TR_LAYER * l
                n0 = FIRST[("ada", l)]
                link(dve.memset(xt_lo[:, :, 0:66].bitcast(F32), 0.0))
                dve.memset(xt_hi[:, :, 0:66].bitcast(F32), 0.0).then_inc(cs_ready, 1)
                dve.wait_ge(cs_ready, 2 * l + 2)
                dve.tensor_copy(xt_lo[:, :, 0], xt_hi[:, :, 0].bitcast(F32)).then_inc(dve_step, 1)
                steps[0] += 1
                dve.tensor_tensor(xt_hi[:, :, 1], c_act[:, :], xt_hi[:, :, 0].bitcast(F32), ALU.subtract)\
                   .then_inc(c_ready, 1)

                def mod_in(a):
                    m = 6 * l + a
                    dve.wait_ge(mod_psum, m + 1)
                    if a % 3 == 0:
                        dve.tensor_copy(shift[:, a // 3, :], ps(4)[:, 0:KD]).then_inc(mod_done, 1)
                    elif a % 3 == 1:
                        dve.scalar_tensor_tensor(scale[:, a // 3, :], ps(4)[:, 0:KD], 1.0, gains[:, 2 * l + a // 3, :],
                                                 ALU.add, ALU.mult).then_inc(mod_done, 1)
                    else:
                        dve.wait_ge(in_gain, 32 * (l + 1))
                        dve.tensor_tensor(G[:, a // 3, :], pair(2), G[:, a // 3, :], ALU.mult).then_inc(mod_done, 1)

                for n in range(n0, n0 + 24):
                    static_split(n)
                    i = n - n0
                    if i % 4 == 2 and i > 4:
                        mod_in(i // 4 - 1)
                mod_in(5)
                variance(norm, D); norm += 1
                normed(xn_mix)
                dve.wait_ge(mod_done, 6 * (l + 1))
                modulated(l, 0, tr + TR_H, None)
                n0 = FIRST[("win", l)]

                def win_out(n):
                    _, _, g, h = SLABS[n]
                    if h == 0:
                        return
                    dve.wait_ge(pe_done, n + 1)
                    src = bank[g % 2][:, 1, :]
                    if g < QK_GROUPS:
                        cb = 4 * g + 2
                        dst, at = (qT, cb) if cb < 6 else (kT, cb - 6)
                        dst = dst[:, at:at + 2, :].rearrange("p c n -> p (c n)")
                        dve.tensor_scalar(dst, src, 0.125 if cb < 6 else 1.0, None, ALU.mult).then_inc(ev_dve, 1)
                    else:
                        w = min(512, NAT_COLS - (g - QK_GROUPS) * 512)
                        at = (g - QK_GROUPS) * 512
                        dve.tensor_copy(nat[:, 1, at:at + w], src[:, 0:w]).then_inc(ev_dve, 1)

                for n in range(n0, n0 + 29):
                    static_split(n)
                    if n > n0:
                        win_out(n - 1)
                win_out(n0 + 28)
                dve.wait_ge(in_table, 16 * (l + 1))
                dve.wait_ge(rot_done, l + 1)

                def group_out(j):
                    if j >= 0 and j % HG == HG - 1:
                        dve.wait_ge(pv_psum, HEADS * l + j + 1)
                        g = j // HG
                        dve.tensor_copy(og[:, g, :, :].rearrange("p t n -> p (t n)"), ps(2 + g % 2)).then_inc(og_done, 1)

                for i in range(HEADS):
                    h = HEADS * l + i
                    g, hh = divmod(i, HG)
                    dve.wait_ge(sc_psum, h + 1)
                    if h >= 2:
                        dve.wait_ge(pT_psum, h - 1)
                    o = ps(4 + i % 2)
                    pr = probs[:, i % 2, :]
                    dve.scalar_tensor_tensor(pr[:, 0:P], dist[:, g, P:2 * P], -SLOPES[i], o[:, 0:P], ALU.mult, ALU.add)
                    link(dve.scalar_tensor_tensor(pr[:, P:3 * P], dist[:, g, :], -SLOPES[i], o[:, P:3 * P],
                                                  ALU.mult, ALU.add))
                    link(dve.tensor_reduce(neg_max[:, g, hh, 0:1], pr[:, 0:P], AX, ALU.max, negate=True))
                    dve.tensor_reduce(neg_max[:, g, hh, 1:2], pr[:, P:3 * P], AX, ALU.max, negate=True)\
                       .then_inc(sm_ready, 1)
                    group_out(i - 2)
                group_out(HEADS - 2)
                group_out(HEADS - 1)
                dve.wait_ge(ln_ready, l + 1)
                dve.wait_ge(sm_ready, HEADS * (l + 1))
                flat = lambda a: a.rearrange("p h t -> p (h t)")
                link(dve.tensor_tensor(lse[:, :, :, :], lse[:, :, :, :], neg_max[:, :, :, :], ALU.subtract))
                link(dve.tensor_tensor(top[:, :, :], lse[:, 0, :, :], lse[:, 1, :, :], ALU.max))
                link(dve.tensor_tensor(top[:, :, :], top[:, :, :], lse[:, 2, :, :], ALU.max))
                for g in range(GROUPS):
                    ins = dve.tensor_tensor(lse[:, g, :, :], lse[:, g, :, :], top[:, :, :], ALU.subtract)
                    ins.then_inc(lse_ready, 1) if g == GROUPS - 1 else link(ins)
                link(dve.reciprocal(den[:, :, :, :], den[:, :, :, :]))
                dve.wait_ge(ex_ready, l + 1)
                link(dve.tensor_tensor(top[:, :, :], coef[:, 0, :, :], coef[:, 1, :, :], ALU.add))
                link(dve.tensor_tensor(top[:, :, :], top[:, :, :], coef[:, 2, :, :], ALU.add))
                link(dve.reciprocal(top[:, :, :], top[:, :, :]))
                link(dve.tensor_tensor(coef[:, :, :, :], coef[:, :, :, :], den[:, :, :, :], ALU.mult))
                for g in range(GROUPS):
                    link(dve.tensor_tensor(coef[:, g, :, :], coef[:, g, :, :], top[:, :, :], ALU.mult))
                dve.wait_ge(og_done, GROUPS * (l + 1))
                for g in range(GROUPS):
                    for t in range(TILES):
                        v = og[:, g, t, :].rearrange("p (h n) -> p h n", h=HG)
                        w = coef[:, g, :, t:t + 1].to_broadcast([P, HG, DH])
                        link(dve.tensor_tensor(v, v, w, ALU.mult))
                link(dve.tensor_tensor(og[:, 0, :, :], og[:, 0, :, :], og[:, 1, :, :], ALU.add))
                dve.tensor_tensor(og[:, 0, :, :], og[:, 0, :, :], og[:, 2, :, :], ALU.add).then_inc(att_ready, 1)
                for s in range(4):
                    dst, at = ((qrT, 2 * s) if s < 2 else (krT, 2 * s - 4))
                    step = tr + TR_RQ + s
                    dve.wait_ge(tr_psum, step + 1)
                    dve.tensor_scalar(dst[:, at:at + 2, :].rearrange("p c n -> p (c n)"), ps(6 + step % 2),
                                      1.0 if s < 2 else RDK ** -0.5, None, ALU.mult).then_inc(tr_done, 1)
                for i in range(RH + 1):
                    if i < RH:
                        r = RH * l + i
                        dve.wait_ge(rs_psum, r + 1)
                        dve.wait_ge(dec_ready, r + 1)
                        if i < 2:
                            dve.wait_ge(pT_psum, HEADS * (l + 1))
                        else:
                            dve.wait_ge(ro_psum, r - 1)
                        o = ps(4 + i % 2)
                        pr = probs[:, i % 2, :]
                        link(dve.tensor_tensor(pr[:, 0:T], o[:, 0:T], decay[:, :], ALU.mult))
                        dve.tensor_tensor(pr[:, T:T + P], o[:, T:T + P], decay[:, 0:P], ALU.mult).then_inc(rp_ready, 1)
                    if i >= 1:
                        j = i - 1
                        dve.wait_ge(ro_psum, RH * l + j + 1)
                        dve.tensor_copy(nat[:, :, QR + j * RDV:QR + (j + 1) * RDV],
                                        ps(2 + j % 2)[:, 0:T].rearrange("p (t n) -> p t n", t=TILES)).then_inc(ro_done, 1)
                dve.wait_ge(ro_done, RH * (l + 1))
                dve.wait_ge(sc_psum, HEADS * (l + 1))
                for t in range(TILES):
                    rt = nat[:, t, QR:QR + D]
                    link(dve.tensor_tensor(scratch, rt, rt, ALU.mult))
                    link(dve.tensor_reduce(r_sum[:, t, :], scratch.rearrange("p (h n) -> p h n", h=RH), AX, ALU.add))
                dve.tensor_scalar(r_var[:, :, :], r_sum[:, :, :], 1.0 / RDV, EPS, ALU.mult, ALU.add).then_inc(var_ready, 1)
                dve.wait_ge(std_ready, norm + 1)
                norm += 1
                link(dve.reciprocal(r_sum[:, :, :], r_std[:, :, :]))
                dve.wait_ge(gates_ready, 2 * TILES * (l + 1))
                for t in range(TILES):
                    rt = nat[:, t, QR:QR + D]
                    link(dve.tensor_tensor(rt, rt, nat[:, t, GR:GR + D], ALU.mult))
                    v = rt.rearrange("p (h n) -> p h n", h=RH)
                    ins = dve.tensor_tensor(v, v, r_sum[:, t, :].unsqueeze(2).to_broadcast([P, RH, RDV]), ALU.mult)
                    ins.then_inc(ret_ready, 1) if t == TILES - 1 else link(ins)
                n = FIRST[("att", l)]
                plain(tr + TR_ATT, 1)
                static_split(n)
                dve.wait_ge(pe_done, n + 1)
                for t in range(TILES):
                    v = nat[:, t, GA:GA + D]
                    ins = dve.tensor_tensor(v, v, pair(t), ALU.mult)
                    ins.then_inc(mrg_att, 1) if t == TILES - 1 else link(ins)
                plain(tr + TR_RET, 4)
                for q in range(4):
                    static_split(n + 1 + q)
                dve.wait_ge(pe_done, n + 5)
                dve.wait_ge(mrg_att, l + 1)
                for t in range(TILES):
                    v, w = nat[:, t, GA:GA + D], nat[:, t, GB:GB + D]
                    link(dve.tensor_tensor(w, w, pair(t), ALU.mult))
                    ins = dve.tensor_tensor(v, v, w, ALU.add)
                    ins.then_inc(mrg_ready, 1) if t == TILES - 1 else link(ins)
                plain(tr + TR_MIX, 4)
                for q in range(4):
                    static_split(n + 5 + q)
                variance(norm, D); norm += 1
                add_norm(l, 0, [pair(t) for t in range(TILES)], scratch)
                variance(norm, D); norm += 1
                normed(h_nat)
                if l == LAYERS - 1:
                    modulated(l, 1, tr + TR_H2, hT)
                else:
                    modulated(l, 1, tr + TR_H2, None)
                    for k in range(PASS):
                        static_split(FFN0 + k)
                        if k:
                            ffn_task(k - 1, TILES, 0)
                    variance(norm, D); norm += 1
                    add_norm(l, 1, [pair(2 + t) for t in range(TILES)], h_nat[:, 0, :])

            for s in range(4):
                step = 2 * TR_LAYER + s
                dve.wait_ge(tr_psum, step + 1)
                for kk in range(2):
                    dst = h_nat[:, :, (2 * s + kk) * P:(2 * s + kk + 1) * P]
                    src = ps(6 + step % 2)[:, kk * T:(kk + 1) * T].rearrange("p (t n) -> p t n", t=TILES)
                    ins = dve.tensor_copy(dst, src)
                    ins.then_inc(tr_done, 1) if kk else None
            for t in range(TILES):
                dve.wait_ge(lg_psum, t + 1)
                link(dve.tensor_tensor(logits[:, t, :], ps(4 + t)[:, 0:EXPERTS], router_b[:, :], ALU.add))
                link(dve.max(best[:, t, :], logits[:, t, :]))
                link(dve.max_index(best_i[:, t, :], best[:, t, :], logits[:, t, :]))
            link(dve.tensor_copy(best_f[:, :, :], best_i[:, :, :]))
            dve.tensor_tensor(gate[:, :, 0], best[:, :, 1], best[:, :, 0], ALU.subtract).then_inc(bd_ready, 1)
            for t in range(TILES):
                for j in range(2):
                    link(dve.tensor_scalar(one_hot[:, t, j, :], iota[:, 0:EXPERTS], best_f[:, t, j:j + 1], None, ALU.is_equal))
            dve.wait_ge(e2_ready, 1)
            link(dve.tensor_scalar(gate[:, :, 0], gate[:, :, 1], 1.0, None, ALU.add))
            link(dve.reciprocal(gate[:, :, 0], gate[:, :, 0]))
            link(dve.tensor_tensor(gate[:, :, 1], gate[:, :, 1], gate[:, :, 0], ALU.mult))
            for t in range(TILES):
                link(dve.tensor_scalar(route[:, t, 2, :], one_hot[:, t, 0, :], gate[:, t, 0:1], None, ALU.mult))
                link(dve.scalar_tensor_tensor(route[:, t, 2, :], one_hot[:, t, 1, :], gate[:, t, 1:2], route[:, t, 2, :],
                                              ALU.mult, ALU.add))
                ins = dve.tensor_tensor(route[:, t, 0, :], one_hot[:, t, 0, :], one_hot[:, t, 1, :], ALU.add)
                ins.then_inc(route_ready, 1) if t == TILES - 1 else link(ins)
            dve.wait_ge(rank_psum, 1)
            for t in range(TILES):
                link(dve.tensor_copy(route[:, t, 1, :], ps(t)[:, 0:EXPERTS]))
            dve.memset(y_sum[:, :, :], 0.0).then_inc(y_added, 4)
            dve.tensor_copy(counts[0:1, :], ps(2)[0:1, 0:EXPERTS]).then_inc(routed, 1)
            dve.wait_ge(routed, 1)
            dve.wait_ge(y_added, 4)

            with dve.Fori(0, EXPERTS) as e:
                slab0 = dve.snap(e * PASS + N_STATIC)
                group0 = dve.snap(e * GF + GF)
                count = dve.value_load(counts[0:1, bass.ds(e, 1)], min_val=0, max_val=T)
                dve.tensor_copy(route_e[:, :, :].rearrange("p t a -> p (t a)"),
                                route[:, :, :, bass.ds(e, 1)].rearrange("p t a e -> p (t a e)")).then_inc(col_ready, 1)
                dve.wait_ge(col_ready, e + 1)
                for t in range(TILES):
                    dve.tensor_scalar(pick[:, t, :], iota, route_e[:, t, 1:2], route_e[:, t, 0:1],
                                      ALU.is_equal, ALU.mult).then_inc(pick_ready, 1)
                dve.wait_ge(pkT_psum, e + 1)
                dve.wait_ge(pkT_ready, e + 1)
                dve.tensor_copy(slot_w[:, :], ps(7)[:, T:T + 1]).then_inc(sw_ready, 1)
                for s in range(2):
                    dve.wait_ge(xg_hi_ready, e * 2 + (s + 1))
                    hi, lo = (b[:, 4 * s:4 * s + 4, :].rearrange("p k n -> p (k n)") for b in (xg_hi, xg_lo))
                    dve.tensor_tensor(lo, ps(6 + s), hi.bitcast(F32), ALU.subtract).then_inc(xg_ready, 1)

                def expert(tiles):
                    for k in range(PASS):
                        dve.wait_ge(hi_done, slab0 + (k + 1))
                        split_lo(N_STATIC + k, k % FFN_SLOTS)
                        if k:
                            ffn_task(k - 1, tiles, group0)

                with dve.If(count > P):
                    expert(TILES)
                    dve.wait_ge(pe_done, slab0 + PASS)
                    dve.sem_inc(yl_ready, 1)
                    for t in range(TILES):
                        dve.scalar_tensor_tensor(y_sum[:, t, :], pair(2 + t), route_e[:, t, 2:3], y_sum[:, t, :],
                                                 ALU.mult, ALU.add).then_inc(y_added, 2)
                with dve.Else():
                    expert(1)
                    dve.wait_ge(yh_ready, e + 1)
                    flat_hi, flat_lo = (b[:, :, :].rearrange("p k n -> p (k n)") for b in (xg_hi, xg_lo))
                    dve.scalar_tensor_tensor(flat_lo, pair(2), slot_w[:, 0:1], flat_hi.bitcast(F32),
                                             ALU.mult, ALU.subtract).then_inc(yl_ready, 1)
                    for i in range(4):
                        t, half = divmod(i, 2)
                        dve.wait_ge(back_psum, e * 4 + (i + 1))
                        y = y_sum[:, t, half * 512:(half + 1) * 512]
                        dve.tensor_tensor(y, y, ps(6 + i % 2), ALU.add).then_inc(y_added, 1)
                dve.wait_ge(y_added, e * 4 + 8)

            variance(norm, D)
            add_norm(LAYERS - 1, 1, [y_sum[:, t, :] for t in range(TILES)], h_nat[:, 0, :])


def kernel(**inputs):
    import numpy as _np
    import concourse.bacc as _bacc
    from concourse import mybir as _mybir
    from concourse.bass_utils import run_bass_kernel_spmd as _run

    mix_table, perm_table = host_constants()
    a = {k: _np.ascontiguousarray(v) for k, v in inputs.items()}
    cols = lambda v: v.reshape(-1, KD, P).transpose(2, 0, 1).reshape(P, -1)
    gain_cols = _np.stack([a["norm_pre_mix"], a["norm_pre_ffn"]], 1)
    laid = [
        ("x", a["x"]), ("c_cols", cols(a["c"])), ("w_ada", a["w_ada"]), ("b_ada", a["b_ada"]), ("w_in", a["w_in"]),
        ("w_att", a["w_att_proj"]), ("w_ret", a["w_ret_proj"]), ("w_mix", a["w_mix_out"]),
        ("gain_cols", cols(gain_cols)), ("post_mix", a["norm_post_mix"]), ("post_ffn", a["norm_post_ffn"]),
        ("w_gate", a["w_ffn_gate"]), ("w_up", a["w_ffn_up"]), ("w_down", a["w_ffn_down"]),
        ("w_router", a["w_router"]), ("b_router", a["b_router"]), ("e_gate", a["w_exp_gate"][0]),
        ("e_up", a["w_exp_up"][0]), ("e_down", a["w_exp_down"][0]), ("mix_table", mix_table), ("perm_table", perm_table),
    ]
    nc = _bacc.Bacc("TRN2", target_bir_lowering=False, num_devices=1)
    arrays, args = {}, []
    for name, v in laid:
        v = _np.ascontiguousarray(v)
        arrays[f"in_{name}_dram"] = v
        args.append(nc.dram_tensor(f"in_{name}_dram", v.shape, _mybir.dt.from_np(v.dtype), kind="ExternalInput").ap())
    out = nc.dram_tensor("out_0_dram", (1, T, D), F32, kind="ExternalOutput").ap()
    hybrid_block_kernel(nc, *args, out)
    r = _run(nc, [arrays], core_ids=[0])
    return r.results[0]["out_0_dram"]
```

```python
from contextlib import ExitStack

import numpy as np
import concourse.bass as bass
from concourse import mybir

F32 = mybir.dt.float32
F32R = mybir.dt.float32r
I32 = mybir.dt.int32
U32 = mybir.dt.uint32
ALU = mybir.AluOpType
ACT = mybir.ActivationFunctionType
AX = mybir.AxisListType.X

P = 128
EPS = 1e-6
INVALID = 1e33

D, T, LAYERS = 1024, 256, 2
TILES = T // P
KD = D // P
HG, GROUPS, DH = 4, 3, 64
HEADS = HG * GROUPS
RH, RDK, RDV = 8, 64, 128
FF = 2816
EXPERTS = 8
GF = FF // 256
IN_COLS = 7424

QK_COLS = 2 * HEADS * DH
NAT_COLS = IN_COLS - QK_COLS
VA, QR, KR, VR, GR, GA, GB = 0, 768, 1280, 1792, 2816, 3840, 4864
WIN_GROUPS = 15
QK_GROUPS = QK_COLS // 512

SLAB = 2048
MIX_SLOTS, FFN_SLOTS, SPLIT_SLOTS = 4, 11, 3
PASS = 3 * GF


def ffn_order():
    order = [("gu", 0, 0), ("gu", 0, 1)]
    for g in range(1, GF):
        order += [("gu", g, 0), ("gu", g, 1), ("dn", g - 1, 0)]
    return order + [("dn", GF - 1, 0)]


FFN_ORDER = ffn_order()


CHUNKS = [(0, 0), (0, 1), (0, 2), (0, 5), (0, 3), (0, 4), (1, 0), (1, 1), (1, 3), (1, 4), (1, 2), (1, 5)]
CHUNK_AT = {c: m for m, c in enumerate(CHUNKS)}
COLUMN_HALVES = [2 * sum(a % 3 < 2 for _, a in CHUNKS[:m]) for m in range(len(CHUNKS))]
MOD_AFTER_WIN = {0: {5: (2, 0), 9: (3, 0), 13: (4, 0), 14: (4, 1), 17: (5, 0), 18: (5, 1)},
                 1: {5: (10, 0), 9: (11, 0)}}
MOD_AFTER_FFN = {8: (6, 0), 11: (6, 1), 14: (7, 0), 17: (7, 1), 20: (8, 0), 23: (8, 1), 29: (9, 0), 31: (9, 1)}
ADA_UNDER_FFN = [1, 3, 5, 7, 9, 11, 12, 13, 15, 17, 18, 19, 21, 23, 25, 27]


WIN_ORDER = [(0, 0), (1, 0), (0, 1), (1, 1)] + [(g, h) for g in range(2, WIN_GROUPS - 1) for h in range(2)]
WIN_ORDER += [(WIN_GROUPS - 1, 1)]
WIN_OUT = {s: g for s, (g, h) in enumerate(WIN_ORDER) if h == 1}


def ada_columns(a):
    if a % 3 == 2:
        return [(a * D, D // 2), (a * D + D // 2, D // 2)]
    base, half = a - a % 3, a % 3
    return [((base + i) * D + half * (D // 2), D // 2) for i in range(2)]


def static_slabs():
    def ada(m):
        return [("ada", CHUNKS[m][0], CHUNKS[m][1], q) for q in range(4)]

    out = ada(0)
    for l in range(LAYERS):
        win = [("win", l, g, h) for g, h in WIN_ORDER]
        under = [s for m in ((2, 3, 4, 5), (10, 11))[l] for s in ada(m)]
        for i, slab in enumerate(win):
            out.append(slab)
            if l == 0 and i < 2:
                out += ada(1)[2 * i:2 * i + 2]
            elif i and under:
                out.append(under.pop(0))
        out += [("att", l, 0, 0)] + [("ret", l, q, 0) for q in range(4)] + [("mix", l, q, 0) for q in range(4)]
        if l == 0:
            under = [s for m in (6, 7, 8, 9) for s in ada(m)]
            for i, (kind, g, h) in enumerate(FFN_ORDER):
                out.append((kind, l, g, h))
                if i in ADA_UNDER_FFN:
                    out.append(under.pop(0))
    return out


SLABS = static_slabs()
N_STATIC = len(SLABS)
FIRST = {}
for _n, _s in enumerate(SLABS):
    FIRST.setdefault(_s[:2], _n)
PRODUCTS = [n for n, s in enumerate(SLABS) if s[0] != "ada"]
NUMBER = {n: m for m, n in enumerate(PRODUCTS)}
M_STATIC = len(PRODUCTS)
WIN_M = [NUMBER[FIRST[("win", l)]] for l in range(LAYERS)]
ATT_M = [NUMBER[FIRST[("att", l)]] for l in range(LAYERS)]
FFN_M = NUMBER[FIRST[("gu", 0)]]
WIN_SLABS = 2 * WIN_GROUPS - 1
ATT_FROM, TURN_FROM, RET_FROM = 10, 20, 24
SILU_AT, ATT_TURN = 23, 27

TR_H, TR_RQ, TR_ATT, TR_RET, TR_MIX, TR_H2 = 0, 4, 8, 9, 13, 17
TR_LAYER = 21

SLOPES = [2.0 ** (-8.0 * (h + 1) / HEADS) for h in range(HEADS)]
LOG_GAMMA = [float(np.log1p(-(2.0 ** (-5.0 - h)))) for h in range(RH)]


def slab_slots():
    slot, before, use, last, count, at, was = [], [], [], {}, {}, 0, False
    f0, f1 = PRODUCTS[FFN_M], PRODUCTS[FFN_M + PASS - 1]
    for n in range(N_STATIC):
        wide = f0 <= n <= f1
        if wide != was:
            at = 0
        was = wide
        j = at % (FFN_SLOTS if wide else MIX_SLOTS)
        at += 1
        count[j] = count.get(j, 0) + 1
        slot.append(j)
        before.append(last.get(j))
        use.append(count[j])
        last[j] = n
    return slot, before, use, last, count


SLOT, BEFORE, USE, LAST_USER, USES = slab_slots()


def host_constants():
    q = np.arange(P)[:, None]
    dist = np.full((P, GROUPS, 2, P), INVALID, np.float32)
    for g, (dil, reach) in enumerate(((1, 128), (4, 512), (16, 2048))):
        for b, shift in enumerate((P, 0)):
            d = q + shift - np.arange(P)[None]
            ok = (d >= 0) & (d <= reach) & (d % dil == 0)
            dist[:, g, b] = np.where(ok, d, INVALID)
    rel = np.full((P, 2, P), INVALID, np.float32)
    for b, shift in enumerate((0, P)):
        d = np.arange(P)[None] + shift - q
        rel[:, b] = np.where(d >= 0, d, INVALID)
    half = RDK // 2
    inv = (1.0 / (np.float32(10000.0) ** (np.arange(half, dtype=np.float32) / np.float32(half)))).astype(np.float32)
    ang = (np.arange(T, dtype=np.float32)[:, None] * inv[None]).astype(np.float32)
    trig = np.stack([np.cos(ang), np.sin(ang)], 1).astype(np.float32)
    trig = trig.reshape(TILES, P, 2 * half).transpose(1, 0, 2).reshape(P, -1)
    mix = np.concatenate([dist.reshape(P, -1), rel.reshape(P, -1), trig], 1)
    ident = np.eye(P, dtype=np.float32)
    iota = np.tile(np.arange(P, dtype=np.float32)[None], (P, 1))
    before = (np.arange(P)[:, None] < np.arange(P)[None]).astype(np.float32)
    perm = np.concatenate([ident, np.ones((P, P), np.float32), iota, before], 1)
    return np.ascontiguousarray(mix, np.float32), np.ascontiguousarray(perm, np.float32)


def slab_rows(w, kind, l, a, b):
    def chunks(m, first, n, cols):
        return m[first * P:(first + n) * P, cols].reshape(n, P, -1).transpose(1, 0, 2)

    if kind == "ada":
        v = np.concatenate([chunks(w["w_ada"][l], 2 * b, 2, slice(at, at + n)) for at, n in ada_columns(a)], 2)
    elif kind == "win":
        last = a == WIN_GROUPS - 1
        v = chunks(w["w_in"][l], 0 if last else 4 * b, KD if last else 4, slice(a * 512, min((a + 1) * 512, IN_COLS)))
    elif kind in ("att", "ret", "mix"):
        v = chunks(w[{"att": "w_att_proj", "ret": "w_ret_proj", "mix": "w_mix_out"}[kind]][l], 2 * a, 2, slice(0, D))
    elif kind == "gu":
        v = np.stack([chunks(w[n], 4 * b, 4, slice(a * 256, (a + 1) * 256)) for n in ("gate", "up")], 2)
    else:
        v = chunks(w["down"], 2 * a, 2, slice(0, D))
    return v.reshape(P, SLAB)


def lay_out_weights(w):
    dense = dict(w, gate=w["w_ffn_gate"][0], up=w["w_ffn_up"][0], down=w["w_ffn_down"][0])
    stream = np.stack([slab_rows(dense, *s) for s in SLABS])
    experts = np.empty((EXPERTS * PASS, P, SLAB), stream.dtype)
    for e in range(EXPERTS):
        one = dict(gate=w["w_exp_gate"][0, e], up=w["w_exp_up"][0, e], down=w["w_exp_down"][0, e])
        for k, (kind, g, h) in enumerate(FFN_ORDER):
            experts[e * PASS + k] = slab_rows(one, kind, 1, g, h)
    return stream, experts


def hybrid_block_kernel(nc, x, c_cols, b_ada, stream, experts, gain_cols, post_mix, post_ffn, w_router, b_router,
                        mix_table, perm_table, out):
    with ExitStack() as ctx:
        def sb(name, shape, dt=F32, where=ctx):
            return where.enter_context(nc.sbuf_tensor(name, shape, dt))

        def sem(name):
            return ctx.enter_context(nc.semaphore(name))

        w_hi = sb("w_hi", [P, SPLIT_SLOTS, SLAB], F32R)
        w_lo = sb("w_lo", [P, SPLIT_SLOTS, SLAB], F32R)
        raw_a = sb("raw_a", [P, MIX_SLOTS, SLAB])
        X = sb("X", [P, TILES, D])
        G = sb("G", [P, 2, D])
        acc0 = sb("acc0", [P, D])
        xt_hi = sb("xt_hi", [P, KD, T], F32R)
        xt_lo = sb("xt_lo", [P, KD, T], F32R)
        perm = sb("perm", [P, 4, P])
        ident, ones, iota, earlier = (perm[:, i, :] for i in range(4))
        c_sb = sb("c_sb", [P, KD])
        c_act = sb("c_act", [P, KD])
        gains = sb("gains", [P, LAYERS * 2, KD])
        shift = sb("shift", [P, LAYERS * 2, KD])
        scale = sb("scale", [P, LAYERS * 2, KD])
        ssum = sb("ssum", [P, TILES])
        var = sb("var", [P, TILES])
        std = sb("std", [P, TILES])
        rstd = sb("rstd", [P, TILES])
        idle = sb("idle", [P, 8])
        in_turn = ExitStack()
        h_tmp = sb("h_tmp", [P, 2, 2, T], where=in_turn)
        in_turn.close()
        att_parts = sb("att_parts", [P, 2, 2, T], F32R)
        router_w = sb("router_w", [P, KD, EXPERTS])
        router_b = sb("router_b", [P, EXPERTS])

        mixer = ExitStack()
        qkT = sb("qkT", [P, HEADS, T], where=mixer)
        qT, kT = qkT[:, 0:HEADS // 2, :], qkT[:, HEADS // 2:, :]
        qrT = sb("qrT", [P, RH // 2, T], where=mixer)
        krT = sb("krT", [P, RH // 2, T], where=mixer)
        og = sb("og", [P, GROUPS, TILES, HG * DH], where=mixer)
        probs = sb("probs", [P, 2, 3 * P], where=mixer)
        probsT = sb("probsT", [P, 2, 3 * P], where=mixer)
        decay = sb("decay", [P, 2, 2 * P], where=mixer)
        table = sb("table", [P, mix_table.shape[1]], where=mixer)
        dist = table[:, 0:GROUPS * 2 * P].rearrange("p (g n) -> p g n", g=GROUPS)
        rel = table[:, GROUPS * 2 * P:(GROUPS + 1) * 2 * P]
        trig = table[:, (GROUPS + 1) * 2 * P:].rearrange("p (t s n) -> p t s n", t=TILES, s=2)
        neg_max = sb("neg_max", [P, GROUPS, HG, TILES], where=mixer)
        den = sb("den", [P, GROUPS, HG, TILES], where=mixer)
        lse = sb("lse", [P, GROUPS, HG, TILES], where=mixer)
        top = sb("top", [P, HG, TILES], where=mixer)
        coef = sb("coef", [P, GROUPS, HG, TILES], where=mixer)
        r_sum = sb("r_sum", [P, TILES, RH], where=mixer)
        r_var, r_std = (v[:, :, :, :].rearrange("p g h t -> p (g h t)")[:, 0:TILES * RH].rearrange("p (t h) -> p t h", t=TILES)
                        for v in (lse, den))
        nat = sb("nat", [P, TILES, NAT_COLS], where=mixer)
        xn_mix = nat[:, 0, 0:TILES * D].rearrange("p (t d) -> p t d", t=TILES)
        rot = nat[:, 0, GA:GA + D].rearrange("p (i n) -> p i n", i=4)
        acc1_mix = nat[:, 1, GB:GB + D]
        sq = qkT[:, 0:8, :].rearrange("p (t c) n -> p t (c n)", t=TILES)
        scratch = qkT[:, 0:4, :].rearrange("p c n -> p (c n)")
        mixer.close()

        h_nat = sb("h_nat", [P, TILES, D])
        y_sum = sb("y_sum", [P, TILES, D])
        att_hi, att_lo = (att_parts[:, i, :, :] for i in range(2))
        act_s, act_m = h_tmp[:, 0, :, :], h_tmp[:, 1, :, :]
        aT_hi = sb("aT_hi", [P, TILES, 256], F32R)
        aT_lo = sb("aT_lo", [P, TILES, 256], F32R)
        xg_hi = sb("xg_hi", [P, KD, P], F32R)
        xg_lo = sb("xg_lo", [P, KD, P], F32R)
        pick = acc0[:, 0:T].rearrange("p (t n) -> p t n", t=TILES)
        pickT = acc0[:, T:2 * T]
        logits = sb("logits", [P, TILES, EXPERTS])
        best = sb("best", [P, TILES, 8])
        best_i = sb("best_i", [P, TILES, 8], U32)
        best_f = sb("best_f", [P, TILES, 8])
        gate = sb("gate", [P, TILES, 2])
        one_hot = sb("one_hot", [P, TILES, 2, EXPERTS])
        route = sb("route", [P, TILES, 3, EXPERTS + 1])
        route_e = sb("route_e", [P, TILES, 3])
        all_w = sb("all_w", [P, TILES])
        slot_w = sb("slot_w", [P, 1])
        counts = sb("counts", [1, EXPERTS], I32)
        raw_b = sb("raw_b", [P, FFN_SLOTS - MIX_SLOTS, SLAB])
        hT = y_sum[:, :, :].rearrange("p t (k n) -> p (t k) n", n=T)

        y_one = G[:, 0, :]

        def acc(m):
            if m % 2 == 0:
                return acc0[:, :]
            return G[:, 0, :] if 6 <= m < 10 else acc1_mix

        def raw(j):
            return raw_a[:, j, :] if j < MIX_SLOTS else raw_b[:, j - MIX_SLOTS, :]

        bank = [ctx.enter_context(nc.psum_tensor(f"ps{i}", [P, 2, 512], F32)) for i in range(4)]

        def ps(i):
            return bank[i // 2][:, i % 2, :]

        def whole(i):
            return ps(i).rearrange("p (t n) -> p t n", t=TILES)

        def pair(i):
            return bank[i][:, :, :].rearrange("p b n -> p (b n)")

        slab_in = [sem(f"slab_in{j}") for j in range(FFN_SLOTS)]
        hi_done, lo_done, pe_done = sem("hi_done"), sem("lo_done"), sem("pe_done")
        in_x, in_c, in_small, in_router, in_table, in_gain, in_bias = (
            sem("in_x"), sem("in_c"), sem("in_small"), sem("in_router"), sem("in_table"), [sem("in_gain0"), sem("in_gain1")], [sem("in_bias0"), sem("in_bias1")])
        dve_step, act_step, pool_step = sem("dve_step"), sem("act_step"), sem("pool_step")
        c_ready, acc_zero, acc_ready, mod_psum, mod_done = (
            sem(n) for n in ("c_ready", "acc_zero", "acc_ready", "mod_psum", "mod_done"))
        mod_turned, first_bias = sem("mod_turned"), sem("first_bias")
        tile_done, r_var_ready, r_std_ready = sem("tile_done"), sem("r_var_ready"), sem("r_std_ready")
        ss_ready, var_ready, std_ready, xn_ready = sem("ss_ready"), sem("var_ready"), sem("std_ready"), sem("xn_ready")
        home_psum, home_done = sem("home_psum"), sem("home_done")
        tr_psum, tr_mod, tr_hi, tr_done = sem("tr_psum"), sem("tr_mod"), sem("tr_hi"), sem("tr_done")
        ev_act, ev_dve = sem("ev_act"), sem("ev_dve")
        rot_done = sem("rot_done")
        sc_psum, sm_ready, p_ready, pT_psum, pT_ready, pv_psum, og_done = (
            sem(n) for n in ("sc_psum", "sm_ready", "p_ready", "pT_psum", "pT_ready", "pv_psum", "og_done"))
        ln_ready, lse_ready, ex_ready, att_ready = sem("ln_ready"), sem("lse_ready"), sem("ex_ready"), sem("att_ready")
        rs_psum, dec_ready, rp_ready, ro_psum, ro_done = (
            sem(n) for n in ("rs_psum", "dec_ready", "rp_ready", "ro_psum", "ro_done"))
        sq_ready, silu_ready, gated, r_rstd_ready = sem("sq_ready"), sem("silu_ready"), sem("gated"), sem("r_rstd_ready")
        gates_ready, ret_ready, mrg_att, mrg_ready = sem("gates_ready"), sem("ret_ready"), sem("mrg_att"), sem("mrg_ready")
        x_done = sem("x_done")
        s_ready, a_ready, aT_psum, aT_hi_ready, aT_ready = (
            sem(n) for n in ("s_ready", "a_ready", "aT_psum", "aT_hi_ready", "aT_ready"))
        lg_psum, bd_ready, e2_ready, route_ready, rank_psum, routed = (
            sem(n) for n in ("lg_psum", "bd_ready", "e2_ready", "route_ready", "rank_psum", "routed"))
        col_ready, pick_ready, pkT_psum, pkT_ready, sw_ready = (
            sem(n) for n in ("col_ready", "pick_ready", "pkT_psum", "pkT_ready", "sw_ready"))
        xg_psum, xg_hi_ready, xg_ready = sem("xg_psum"), sem("xg_hi_ready"), sem("xg_ready")
        y_ready, back_psum, y_added, allw_ready = sem("y_ready"), sem("back_psum"), sem("y_added"), sem("allw_ready")
        out_sem = sem("out_sem")

        def load_slab(sp, j, src):
            sp.dma_start(raw(j), src).then_inc(slab_in[j], 16)

        def turn_bank(step):
            return 7 if TR_RQ <= step % TR_LAYER <= TR_ATT and step < 2 * TR_LAYER else 6 + step % 2

        def head_pair(p):
            return (2 * p, 2 * p + 1)

        block = ctx.enter_context(nc.Block())

        @block.sync
        def _(sp):
            sp.dma_start(c_sb[:, :], c_cols).then_inc(in_c, 16)
            sp.wait_ge(acc_zero, 1)
            for i, (at, n) in enumerate(ada_columns(CHUNKS[0][1])):
                sp.dma_start(acc(0)[0:1, i * n:(i + 1) * n], b_ada[0:1, at:at + n]).then_inc(first_bias, 16)
            for n, (kind, l, a, b) in enumerate(SLABS):
                if n == 1:
                    sp.dma_start(perm[:, :, :], perm_table.rearrange("p (a n) -> p a n", a=4)).then_inc(in_small, 16)
                    sp.dma_start(gains[:, :, :], gain_cols.rearrange("p (a k) -> p a k", a=2 * LAYERS)).then_inc(in_small, 16)
                if n == 3:
                    sp.dma_start(X[:, :, :], x[0].rearrange("(t p) d -> p t d", p=P)).then_inc(in_x, 16)
                if n == PRODUCTS[WIN_M[l] + 4]:
                    if l:
                        sp.wait_ge(x_done, 2 * TILES * l)
                    sp.dma_start(table[:, :], mix_table).then_inc(in_table, 16)
                    if l == 0:
                        sp.dma_start(router_w[:, :, :], w_router[0].rearrange("(k p) e -> p k e", p=P)).then_inc(in_router, 16)
                        sp.dma_start(router_b[:, :], b_router[0].partition_broadcast(P)).then_inc(in_router, 16)
                    if l:
                        sp.wait_ge(mod_psum, 10)
                    for j, post in enumerate((post_mix, post_ffn)):
                        sp.dma_start(G[:, j, :], post[l].partition_broadcast(P)).then_inc(in_gain[j], 16)
                if BEFORE[n] is not None:
                    sp.wait_ge(lo_done, BEFORE[n] + 1)
                if n == PRODUCTS[FFN_M] + MIX_SLOTS:
                    sp.wait_ge(tr_psum, TR_H2)
                load_slab(sp, SLOT[n], stream[n])

            def expert_slabs(e, ks, nth=None, e_from=None):
                for k in ks:
                    if nth == 0:
                        if LAST_USER.get(k) is not None:
                            sp.wait_ge(lo_done, LAST_USER[k] + 1)
                        if k == MIX_SLOTS:
                            sp.wait_ge(tr_psum, TR_LAYER + TR_H2)
                    else:
                        sp.wait_ge(lo_done, e * PASS + (N_STATIC + k - FFN_SLOTS + 1))
                    n = (e if e_from is None else e_from) * PASS + k
                    load_slab(sp, k % FFN_SLOTS, experts[bass.ds(n, 1), :, :].rearrange("a p n -> (a p) n"))

            expert_slabs(0, range(FFN_SLOTS), nth=0)
            with sp.Fori(0, EXPERTS - 1) as e:
                expert_slabs(e, range(FFN_SLOTS, PASS))
                e1 = sp.snap(e + 1)
                expert_slabs(e1, range(FFN_SLOTS))
            expert_slabs(EXPERTS - 1, range(FFN_SLOTS, PASS))
            expert_slabs(EXPERTS, range(2), e_from=0)
            for t in range(TILES):
                sp.wait_ge(x_done, 2 * TILES * LAYERS - TILES + t + 1)
                sp.dma_start(out[0].rearrange("(t p) d -> p t d", p=P)[:, t, :], X[:, t, :]).then_inc(out_sem, 16)
            sp.wait_ge(out_sem, 16 * TILES)

        @block.gpsimd
        def _(pool):
            steps = [0]

            def link(ins):
                steps[0] += 1
                ins.then_inc(pool_step, 1)
                pool.wait_ge(pool_step, steps[0])

            def clear(m):
                l, a = CHUNKS[m]
                if m >= 2:
                    pool.wait_ge(mod_psum, m - 1)
                if m == 7:
                    pool.wait_ge(x_done, TILES)
                pool.memset(acc(m), 0.0).then_inc(acc_zero, 1)
                pool.wait_ge(acc_zero, m + 1)
                if m == 0:
                    return
                for i, (at, n) in enumerate(ada_columns(a)):
                    pool.dma_start(acc(m)[0:1, i * n:(i + 1) * n], b_ada[l:l + 1, at:at + n]).then_inc(in_bias[m % 2], 16)

            for m in range(6):
                clear(m)
            for l in range(LAYERS):
                pool.wait_ge(in_table, 16 * (l + 1))
                pool.wait_ge(ev_act, WIN_GROUPS * l + 7)
                pool.wait_ge(ev_dve, WIN_GROUPS * l + 7)
                for t in range(TILES):
                    cos, sin = (trig[:, t, s:s + 1, :].to_broadcast([P, RH, 32]) for s in range(2))
                    for at in (QR, KR):
                        v = nat[:, t, at:at + 512].rearrange("p (h s n) -> p h s n", h=RH, s=2)
                        r = [rot[:, i, :].rearrange("p (h n) -> p h n", h=RH) for i in range(4)]
                        pool.tensor_tensor(r[0], v[:, :, 0, :], cos, ALU.mult)
                        pool.tensor_tensor(r[1], v[:, :, 1, :], sin, ALU.mult)
                        pool.tensor_tensor(r[2], v[:, :, 0, :], sin, ALU.mult)
                        link(pool.tensor_tensor(r[3], v[:, :, 1, :], cos, ALU.mult))
                        pool.tensor_tensor(v[:, :, 0, :], r[0], r[1], ALU.subtract)
                        ins = pool.tensor_tensor(v[:, :, 1, :], r[2], r[3], ALU.add)
                        if (t, at) == (TILES - 1, KR):
                            ins.then_inc(rot_done, 1)
                        else:
                            link(ins)
                for p in range(RH // 2):
                    pool.wait_ge(ro_done, RH // 2 * l + p + 1)
                    v = nat[:, :, QR + 2 * p * RDV:QR + 2 * (p + 1) * RDV]
                    pool.tensor_tensor(sq[:, :, 2 * p * RDV:2 * (p + 1) * RDV], v, v, ALU.mult).then_inc(sq_ready, 1)
                    if p == 0:
                        pool.wait_ge(silu_ready, TILES * (l + 1))
                    pool.wait_ge(sq_ready, RH // 2 * l + p + 1)
                    g = nat[:, :, GR + 2 * p * RDV:GR + 2 * (p + 1) * RDV]
                    pool.tensor_tensor(v, v, g, ALU.mult).then_inc(gated, 1)
                if l == 0:
                    for m in range(6, 12):
                        if m == 11:
                            pool.wait_ge(x_done, 2 * TILES)
                        clear(m)

        @block.scalar
        def _(act):
            split = [0]

            def high(j, at):
                act.activation(w_hi[:, at % SPLIT_SLOTS, :], raw(j), ACT.Copy).then_inc(hi_done, 1)

            def ahead(m):
                while split[0] <= min(m, M_STATIC - 1):
                    k = split[0]
                    n = PRODUCTS[k]
                    act.wait_ge(slab_in[SLOT[n]], 16 * USE[n])
                    if k >= SPLIT_SLOTS:
                        act.wait_ge(pe_done, k - SPLIT_SLOTS + 1)
                    high(SLOT[n], k)
                    split[0] += 1

            def tr_high(step, dst, src=None):
                if src is None:
                    act.wait_ge(tr_psum, step + 1)
                    src = ps(turn_bank(step))
                act.activation(dst, src, ACT.Copy).then_inc(tr_hi, 1)

            def roots(k, srcs, ready):
                for t, src in enumerate(srcs):
                    ready(t)
                    junk = (h_tmp[:, :, :, :].rearrange("p a b n -> p (a b n)") if t == 0 else
                            xt_hi[:, 0:4, :].rearrange("p k n -> p (k n)"))
                    act.activation(junk, src, ACT.Square, accum_out=ssum[:, t:t + 1]).then_inc(ss_ready, 1)
                    act.wait_ge(var_ready, TILES * k + t + 1)
                    act.activation(std[:, t:t + 1], var[:, t:t + 1], ACT.Sqrt).then_inc(std_ready, 1)

            def table_in(func, i):
                act.activation(idle[:, i:i + 1], c_sb[:, 0:1], func, scale=0.0)

            def product_rows(last, nth):
                def ready(t):
                    if t == 0:
                        act.wait_ge(tile_done, nth)
                    else:
                        act.wait_ge(pe_done, last + 1)
                return ready

            def added(n):
                return lambda t: act.wait_ge(x_done, n + t + 1)

            def ffn_task(k, tiles, m0, group0):
                kind, g, h = FFN_ORDER[k]
                v = bank[g % 2][:, 0:tiles, 0:256]
                if (kind, h) == ("gu", 1):
                    act.wait_ge(pe_done, m0 + (k + 1))
                    if not (isinstance(group0, int) and group0 + g == 0):
                        act.wait_ge(a_ready, group0 + g)
                    act.activation(act_s[:, 0:tiles, :], v, ACT.Silu).then_inc(s_ready, 1)
                if ((kind, h) == ("gu", 0) and g > 0) or (kind, g) == ("dn", GF - 2):
                    q = g - 1 if kind == "gu" else GF - 1
                    act.wait_ge(aT_psum, group0 + (q + 1))
                    v = bank[q % 2][:, 0:tiles, 0:256]
                    act.activation(aT_hi[:, 0:tiles, :], v, ACT.Copy).then_inc(aT_hi_ready, 1)

            def expert_split(k, m0, uses):
                j = k % FFN_SLOTS
                act.wait_ge(slab_in[j], uses + 16 * (USES.get(j, 0) + k // FFN_SLOTS + 1))
                act.wait_ge(pe_done, m0 + (k - SPLIT_SLOTS + 1))
                high(j, M_STATIC + k)

            act.wait_ge(in_c, 16)
            act.activation(c_act[:, :], c_sb[:, :], ACT.Silu).then_inc(c_ready, 1)
            norm = 0
            for l in range(LAYERS):
                tr = TR_LAYER * l
                x_tiles = [X[:, t, :] for t in range(TILES)]
                roots(norm, x_tiles, added(2 * TILES * l - TILES) if l else lambda t: act.wait_ge(in_x, 16)); norm += 1
                if l == 0:
                    ahead(WIN_M[l])

                def modulated_high(s):
                    act.wait_ge(tr_mod, 4 * 2 * l + s + 1)
                    tr_high(tr + TR_H + s, xt_hi[:, 2 * s:2 * s + 2, :], h_tmp[:, s % 2, :, :])

                for s in range(2 if l == 0 else 4):
                    modulated_high(s)

                def win_out(s):
                    if s not in WIN_OUT:
                        return
                    g = WIN_OUT[s]
                    act.wait_ge(pe_done, WIN_M[l] + s + 1)
                    src = bank[g % 2][:, 0, :]
                    if g < QK_GROUPS:
                        dst = qkT[:, 4 * g:4 * g + 2, :].rearrange("p c n -> p (c n)")
                        act.activation(dst, src, ACT.Copy, scale=(DH ** -0.5 if 4 * g < 6 else 1.0)).then_inc(ev_act, 1)
                    else:
                        at = (g - QK_GROUPS) * 512
                        w = min(512, NAT_COLS - at)
                        act.activation(nat[:, 0, at:at + w], src[:, 0:w], ACT.Copy).then_inc(ev_act, 1)

                def attention(i):
                    h = HEADS * l + i
                    if i < HEADS:
                        g, hh = divmod(i, HG)
                        act.wait_ge(sm_ready, h + 1)
                        for t in range(TILES):
                            v = probs[:, i % 2, 0:P] if t == 0 else probs[:, i % 2, P:3 * P]
                            act.activation(v, v, ACT.Exp, bias=neg_max[:, g, hh, t:t + 1],
                                           accum_out=den[:, g, hh, t:t + 1]).then_inc(p_ready, 1)
                    if 1 <= i <= HEADS:
                        act.wait_ge(pT_psum, h)
                        if h >= 3:
                            act.wait_ge(pv_psum, h - 2)
                        act.activation(probsT[:, (i - 1) % 2, :], ps(5)[:, 0:3 * P], ACT.Copy).then_inc(pT_ready, 1)

                def gates(at):
                    for t in range(TILES):
                        v = nat[:, t, at:at + D]
                        act.activation(v, v, ACT.Sigmoid).then_inc(gates_ready, 1)

                for s in range(WIN_SLABS):
                    if l == 0 and s == 1:
                        modulated_high(2)
                        modulated_high(3)
                    ahead(WIN_M[l] + s + 2)
                    win_out(s)
                    if ATT_FROM <= s < ATT_FROM + HEADS + 1:
                        attention(s - ATT_FROM)
                    if s == SILU_AT:
                        act.wait_ge(ev_act, WIN_GROUPS * l + SILU_AT // 2)
                        act.wait_ge(ev_dve, WIN_GROUPS * l + SILU_AT // 2)
                        for t in range(TILES):
                            v = nat[:, t, GR:GR + D]
                            act.activation(v, v, ACT.Silu).then_inc(silu_ready, 1)
                    if s == RET_FROM:
                        act.wait_ge(p_ready, 2 * HEADS * (l + 1))
                        act.activation(lse[:, :, :, :], den[:, :, :, :], ACT.Ln).then_inc(ln_ready, 1)
                    if RET_FROM <= s < RET_FROM + RH // 2:
                        p = s - RET_FROM
                        for i in head_pair(p):
                            if RH * l + i >= 2:
                                act.wait_ge(rp_ready, RH * l + i - 1)
                            act.activation(decay[:, i % 2, :], rel, ACT.Exp, scale=LOG_GAMMA[i]).then_inc(dec_ready, 1)
                    if s == ATT_TURN:
                        tr_high(tr + TR_ATT, att_hi)
                    if s == RET_FROM + 1:
                        act.wait_ge(lse_ready, l + 1)
                        act.activation(coef[:, :, :, :], lse[:, :, :, :], ACT.Exp).then_inc(ex_ready, 1)
                act.wait_ge(ev_act, WIN_GROUPS * (l + 1))
                act.wait_ge(ev_dve, WIN_GROUPS * (l + 1))
                gates(GA)
                table_in(ACT.Sqrt, 5 + l)
                act.wait_ge(r_var_ready, l + 1)
                act.activation(r_std[:, :, :], r_var[:, :, :], ACT.Sqrt).then_inc(r_std_ready, 1)
                act.wait_ge(r_rstd_ready, l + 1)
                act.wait_ge(gated, RH // 2 * (l + 1))
                for h in range(RH):
                    v = nat[:, 0, QR + h * RDV:QR + (h + 1) * RDV]
                    ins = act.activation(v, v, ACT.Copy, scale=r_sum[:, 0, h:h + 1])
                ins.then_inc(ret_ready, 1)
                for s in range(4):
                    tr_high(tr + TR_RET + s, xt_hi[:, 2 * s:2 * s + 2, :])
                ahead(ATT_M[l] + 3)
                gates(GB)
                table_in(ACT.Sqrt, l)
                ahead(ATT_M[l] + 6)
                for s in range(4):
                    tr_high(tr + TR_MIX + s, xt_hi[:, 2 * s:2 * s + 2, :])
                ahead(ATT_M[l] + 10)
                if l == LAYERS - 1:
                    for k in range(2):
                        expert_split(k, M_STATIC, 0)
                roots(norm, [pair(t) for t in range(TILES)], product_rows(ATT_M[l] + 8, 3 * l + 2)); norm += 1
                roots(norm, x_tiles, added(2 * TILES * l)); norm += 1
                if l == LAYERS - 1:
                    table_in(ACT.Exp, 3)
                for s in range(4):
                    act.wait_ge(tr_mod, 4 * (2 * l + 1) + s + 1)
                    src = h_tmp[:, s % 2, :, :] if l == 0 else hT[:, 2 * s:2 * s + 2, :]
                    tr_high(tr + TR_H2 + s, xt_hi[:, 2 * s:2 * s + 2, :], src)
                if l == 0:
                    for k in range(PASS):
                        ahead(FFN_M + k + 2)
                        ffn_task(k, TILES, FFN_M, 0)
                        if k == PASS - 3:
                            table_in(ACT.Sqrt, 2)
                    roots(norm, [pair(2 + t) for t in range(TILES)], product_rows(FFN_M + PASS - 1, 3)); norm += 1

            for s in range(4):
                act.wait_ge(home_psum, s + 1)
                src = ps(6 + s % 2).rearrange("p (k t n) -> p k t n", k=2, t=TILES)
                dst = h_nat[:, :, 2 * s * P:(2 * s + 2) * P].rearrange("p t (k n) -> p k t n", k=2)
                act.activation(dst, src, ACT.Copy).then_inc(home_done, 1)
                if s == 1:
                    act.wait_ge(bd_ready, 1)
                    act.activation(gate[:, :, 1], gate[:, :, 0], ACT.Exp).then_inc(e2_ready, 1)

            def gathered_high(value):
                for i in range(2):
                    act.wait_ge(xg_psum, value + (i + 1))
                    dst = xg_hi[:, 4 * i:4 * i + 4, :].rearrange("p k n -> p (k n)")
                    act.activation(dst, ps(2 + i), ACT.Copy).then_inc(xg_hi_ready, 1)

            act.wait_ge(routed, 1)
            gathered_high(0)

            with act.Fori(0, EXPERTS) as e:
                m0 = act.snap(e * PASS + M_STATIC)
                group0 = act.snap(e * GF + GF)
                uses = act.snap(e * (16 * (PASS // FFN_SLOTS)))
                count = act.value_load(counts[0:1, bass.ds(e, 1)], min_val=0, max_val=T)

                def expert(tiles):
                    turned = 3 if tiles == TILES else 6
                    for k in range(PASS):
                        expert_split(k + 2, m0, uses)
                        ffn_task(k, tiles, m0, group0)
                        if k == turned:
                            act.wait_ge(pkT_psum, e + 1)
                            act.activation(pickT[:, :], ps(7)[:, 0:T], ACT.Copy).then_inc(pkT_ready, 1)
                        if k == PASS - 2:
                            gathered_high(e * 2 + 2)

                with act.If(count > P):
                    expert(TILES)
                with act.Else():
                    expert(1)
                    act.wait_ge(pe_done, m0 + PASS)
                    act.wait_ge(sw_ready, e + 1)
                    act.activation(y_one, pair(2), ACT.Copy, scale=slot_w[:, 0:1]).then_inc(y_ready, 3)

            table_in(ACT.Sqrt, 4)
            roots(norm, [y_sum[:, t, :] for t in range(TILES)],
                  lambda t: act.wait_ge(y_added, 4 * (EXPERTS + 1) + 2 * (t + 1)))

        @block.tensor
        def _(pe):
            def product(outs, xs, m_at, col, width, first, last):
                whi = w_hi[:, m_at % SPLIT_SLOTS, col:col + width]
                wlo = w_lo[:, m_at % SPLIT_SLOTS, col:col + width]
                for o, (xh, xl) in zip(outs, xs):
                    pe.matmul(o, xh, whi, start=first, stop=False)
                    pe.matmul(o, xh, wlo, start=False, stop=False)
                    ins = pe.matmul(o, xl, whi, start=False, stop=last)
                return ins

            def xt(t, k):
                return xt_hi[:, k, t * P:(t + 1) * P], xt_lo[:, k, t * P:(t + 1) * P]

            def slab_ready(m):
                pe.wait_ge(lo_done, PRODUCTS[m] + 1)

            def last_rows(k_xs, m, bank0):
                for t in range(TILES):
                    for i in range(2):
                        for half in range(2):
                            ins = product([ps(bank0 + 2 * t + half)], [k_xs(t, i)], m, i * 1024 + half * 512, 512,
                                          False, i == 1)
                    if t == 0:
                        ins.then_inc(tile_done, 1)
                ins.then_inc(pe_done, 1)

            def rows_slab(m, q, total, step, x_of=xt):
                pe.wait_ge(tr_done, step + 1)
                slab_ready(m)
                for i in range(2):
                    k = 2 * q + i
                    for half in range(2):
                        outs = [ps(2 * t + half) for t in range(TILES)]
                        ins = product(outs, [x_of(t, k) for t in range(TILES)], m, i * 1024 + half * 512, 512,
                                      k == 0, k == total - 1)
                ins.then_inc(pe_done, 1)

            def turn(step, blocks, read=None):
                if read is not None:
                    pe.wait_ge(tr_mod, read)
                elif step >= 2:
                    pe.wait_ge(tr_done, step if turn_bank(step) == turn_bank(step - 1) else step - 1)
                for i, src in enumerate(blocks):
                    ins = pe.transpose(ps(turn_bank(step))[:, i * P:(i + 1) * P], src, ident)
                ins.then_inc(tr_psum, 1)

            def turn_all(step0, src):
                for s in range(4):
                    turn(step0 + s, [src(t, 2 * s + kk) for kk in range(2) for t in range(TILES)])

            def mod_sum(m, i, at=None, read=None):
                pe.wait_ge(acc_ready, m + 1)
                read = 2 * m + i if read is None else read
                if read:
                    pe.wait_ge(mod_done, read)
                if CHUNKS[m][1] % 3 == 2:
                    for half in range(2):
                        ins = pe.matmul(ps(6 + half), ones, acc(m)[:, half * 512:(half + 1) * 512], start=True, stop=True)
                    ins.then_inc(mod_psum, 1)
                    return
                at = whole(7) if at is None else at
                for b in range(4):
                    k = 4 * i + b
                    ins = pe.transpose(at[:, b // 2, b % 2 * P:(b % 2 + 1) * P], acc(m)[:, k * P:(k + 1) * P], ident)
                ins.then_inc(mod_turned, 1)
                if i:
                    pe.wait_ge(mod_turned, COLUMN_HALVES[m] + 2)
                    pe.sem_inc(mod_psum, 1)

            def ffn(tiles, m_at, ready, group_value, x_of, after=None, sum_under=None):
                for k, (kind, g, h) in enumerate(FFN_ORDER):
                    if kind == "gu" and h == 0 and g >= 2:
                        pe.wait_ge(aT_ready, group_value + (g - 1))
                    ready(k)
                    if kind == "gu":
                        for kk in range(4):
                            kc = 4 * h + kk
                            ins = product([ps(2 * (g % 2) + t) for t in range(tiles)],
                                          [x_of(t, kc) for t in range(tiles)], m_at + k, kk * 512, 512, kc == 0, kc == KD - 1)
                    else:
                        pe.wait_ge(aT_ready, group_value + (g + 1))
                        for i in range(2):
                            xs = [(aT_hi[:, t, i * P:(i + 1) * P], aT_lo[:, t, i * P:(i + 1) * P]) for t in range(tiles)]
                            if sum_under and g == GF - 1:
                                continue
                            for half in range(2):
                                ins = product([ps(4 + 2 * t + half) for t in range(tiles)], xs, m_at + k,
                                              i * 1024 + half * 512, 512, g == 0 and i == 0, g == GF - 1 and i == 1)
                    if sum_under and (kind, g) == ("dn", GF - 1):
                        last_rows(lambda t, i: (aT_hi[:, t, i * P:(i + 1) * P], aT_lo[:, t, i * P:(i + 1) * P]), m_at + k, 4)
                    else:
                        ins.then_inc(pe_done, 1)
                    if (kind == "gu" and h == 0 and g > 0) or (kind == "dn" and g == GF - 2):
                        q = g - 1 if kind == "gu" else GF - 1
                        pe.wait_ge(a_ready, group_value + (q + 1))
                        if sum_under:
                            sum_under(k, q)
                        for t in range(tiles):
                            for i in range(2):
                                ins = pe.transpose(ps(2 * (q % 2) + t)[:, i * P:(i + 1) * P],
                                                   act_m[:, t, i * P:(i + 1) * P], ident)
                        ins.then_inc(aT_psum, 1)
                    if after:
                        after(k)

            def logits_of(s):
                if s == 0:
                    pe.wait_ge(in_router, 32)
                pe.wait_ge(tr_mod, 4 * (2 * LAYERS - 1) + s + 1)
                for k in (2 * s, 2 * s + 1):
                    for t in range(TILES):
                        ins = pe.matmul(ps(4 + t)[:, 0:EXPERTS], hT[:, k, t * P:(t + 1) * P], router_w[:, k, :],
                                        start=(k == 0), stop=(k == KD - 1))
                if s == 3:
                    ins.then_inc(lg_psum, 1)

            pe.wait_ge(in_small, 16 * 2)
            for l in range(LAYERS):
                tr = TR_LAYER * l
                def turn_x(s):
                    turn(tr + TR_H + s, [xn_mix[:, t, (2 * s + kk) * P:(2 * s + kk + 1) * P]
                                         for kk in range(2) for t in range(TILES)],
                         read=8 * l + s - 1 if s >= 2 else None)

                if l == 0:
                    for i in range(2):
                        mod_sum(0, i, whole(4 + i), read=0)
                pe.wait_ge(xn_ready, 2 * TILES * l + TILES)
                for s in range(2 if l == 0 else 4):
                    turn_x(s)

                def win(s):
                    g, h = WIN_ORDER[s]
                    b2 = g % 2
                    m = WIN_M[l] + s
                    if g >= 2 and (h == 0 or g == WIN_GROUPS - 1):
                        pe.wait_ge(ev_act, WIN_GROUPS * l + g - 1)
                        pe.wait_ge(ev_dve, WIN_GROUPS * l + g - 1)
                    if s in (0, 2):
                        pe.wait_ge(tr_done, tr + TR_H + s + 2)
                    slab_ready(m)
                    at = m % SPLIT_SLOTS
                    if g < QK_GROUPS:
                        for kk in range(4):
                            k = 4 * h + kk
                            for b in range(4):
                                o = bank[b2][:, b // 2, (b % 2) * T:(b % 2 + 1) * T]
                                wh = w_hi[:, at, kk * 512 + b * P:kk * 512 + (b + 1) * P]
                                wl = w_lo[:, at, kk * 512 + b * P:kk * 512 + (b + 1) * P]
                                pe.matmul(o, wh, xt_hi[:, k, :], start=(k == 0 and b % 2 == 0), stop=False,
                                          skip_group_check=True)
                                pe.matmul(o, wh, xt_lo[:, k, :], start=False, stop=False, skip_group_check=True)
                                ins = pe.matmul(o, wl, xt_hi[:, k, :], start=False, stop=(k == KD - 1),
                                                skip_group_check=True)
                    elif g < WIN_GROUPS - 1:
                        for kk in range(4):
                            k = 4 * h + kk
                            ins = product([ps(2 * b2 + t) for t in range(TILES)], [xt(t, k) for t in range(TILES)], m,
                                          kk * 512, 512, k == 0, k == KD - 1)
                    else:
                        for k in range(KD):
                            ins = product([ps(2 * b2 + t)[:, 0:256] for t in range(TILES)],
                                          [xt(t, k) for t in range(TILES)], m, k * 256, 256, k == 0, k == KD - 1)
                    ins.then_inc(pe_done, 1)

                def attention(i):
                    if i < HEADS:
                        h = HEADS * l + i
                        pr = slice(64 * (i % 2), 64 * (i % 2) + 64)
                        if h:
                            pe.wait_ge(sm_ready, h)
                        o = ps(4)
                        pe.matmul(o[:, 0:P], qT[pr, i // 2, 0:P], kT[pr, i // 2, 0:P], start=True, stop=True)
                        pe.matmul(o[:, P:3 * P], qT[pr, i // 2, P:T], kT[pr, i // 2, :], start=True, stop=True)\
                          .then_inc(sc_psum, 1)
                    if 1 <= i <= HEADS:
                        j = i - 1
                        h = HEADS * l + j
                        pe.wait_ge(p_ready, 2 * h + 2)
                        if h:
                            pe.wait_ge(pT_ready, h)
                        for b in range(3):
                            ins = pe.transpose(ps(5)[:, b * P:(b + 1) * P], probs[:, j % 2, b * P:(b + 1) * P], ident)
                        ins.then_inc(pT_psum, 1)
                    if i >= 2:
                        j = i - 2
                        h = HEADS * l + j
                        g, hh = divmod(j, HG)
                        pe.wait_ge(pT_ready, h + 1)
                        if hh == 0 and g + l:
                            pe.wait_ge(og_done, GROUPS * l + g)
                        o = ps(6).rearrange("p (t n) -> p t n", t=TILES)
                        v = [nat[:, t, VA + j * DH:VA + (j + 1) * DH] for t in range(TILES)]
                        w = probsT[:, j % 2, :]
                        pe.matmul(o[:, 0, hh * DH:(hh + 1) * DH], w[:, 0:P], v[0], start=True, stop=True)
                        pe.matmul(o[:, 1, hh * DH:(hh + 1) * DH], w[:, P:2 * P], v[0], start=True, stop=False)
                        pe.matmul(o[:, 1, hh * DH:(hh + 1) * DH], w[:, 2 * P:3 * P], v[1], start=False, stop=True)\
                          .then_inc(pv_psum, 1)

                def retention(p):
                    if p >= 1:
                        pe.wait_ge(rp_ready, RH * l + 2 * p)
                        if p >= 2:
                            pe.wait_ge(ro_done, RH // 2 * l + p - 1)
                        for i in head_pair(p - 1):
                            o = ps(6)[:, (i % 2) * T:(i % 2 + 1) * T]
                            v = [nat[:, t, VR + i * RDV:VR + (i + 1) * RDV] for t in range(TILES)]
                            w = probs[:, i % 2, :]
                            pe.matmul(o[:, 0:P], w[:, 0:P], v[0], start=True, stop=True)
                            pe.matmul(o[:, P:2 * P], w[:, P:2 * P], v[0], start=True, stop=False)
                            ins = pe.matmul(o[:, P:2 * P], w[:, 2 * P:3 * P], v[1], start=False, stop=True)
                        ins.then_inc(ro_psum, 1)
                    if p < RH // 2:
                        for i in head_pair(p):
                            pr = slice(64 * (i % 2), 64 * (i % 2) + 64)
                            o = ps(4 + i % 2)
                            pe.matmul(o[:, 0:T], krT[pr, i // 2, 0:P], qrT[pr, i // 2, :], start=True, stop=True)
                            pe.matmul(o[:, T:T + P], krT[pr, i // 2, P:T], qrT[pr, i // 2, P:T], start=True, stop=True)\
                              .then_inc(rs_psum, 1)

                for s in range(WIN_SLABS):
                    win(s)
                    if l == 0 and s == 1:
                        for i in range(2):
                            mod_sum(1, i, whole(4 + i), read=2)
                        turn_x(2)
                        turn_x(3)
                    if s in MOD_AFTER_WIN[l]:
                        mod_sum(*MOD_AFTER_WIN[l][s])
                    if s == ATT_FROM:
                        pe.wait_ge(ev_act, WIN_GROUPS * l + 5)
                        pe.wait_ge(ev_dve, WIN_GROUPS * l + 5)
                    if s == ATT_FROM + 2 and l == 0:
                        pe.wait_ge(mod_done, 8)
                    if ATT_FROM <= s < ATT_FROM + HEADS + 2:
                        attention(s - ATT_FROM)
                    if TURN_FROM <= s < TURN_FROM + 4:
                        i = s - TURN_FROM
                        if i == 0:
                            pe.wait_ge(rot_done, l + 1)
                            pe.wait_ge(mod_done, 12 if l == 0 else 24)
                        at = (QR, KR)[i // 2]
                        turn(tr + TR_RQ + i, [nat[:, t, at + (2 * (i % 2) + kk) * P:at + (2 * (i % 2) + kk + 1) * P]
                                              for kk in range(2) for t in range(TILES)])
                    if s >= RET_FROM:
                        if s == RET_FROM:
                            pe.wait_ge(tr_done, tr + TR_RQ + 4)
                            pe.wait_ge(sm_ready, HEADS * (l + 1))
                            pe.wait_ge(ev_act, WIN_GROUPS * l + 9)
                            pe.wait_ge(ev_dve, WIN_GROUPS * l + 9)
                        if s == RET_FROM + 1:
                            pe.wait_ge(og_done, GROUPS * (l + 1))
                        retention(s - RET_FROM)
                    if s == ATT_TURN:
                        pe.wait_ge(att_ready, l + 1)
                        turn(tr + TR_ATT, [og[:, 0, t, kk * P:(kk + 1) * P] for kk in range(2) for t in range(TILES)])
                m = ATT_M[l]
                pe.wait_ge(ev_act, WIN_GROUPS * (l + 1))
                pe.wait_ge(ev_dve, WIN_GROUPS * (l + 1))
                rows_slab(m, 0, 2, tr + TR_ATT,
                          lambda t, k: (att_hi[:, k, t * P:(t + 1) * P], att_lo[:, k, t * P:(t + 1) * P]))
                pe.wait_ge(ro_done, RH // 2 * (l + 1))
                pe.wait_ge(ret_ready, TILES * (l + 1))
                turn_all(tr + TR_RET, lambda t, k: nat[:, t, QR + k * P:QR + (k + 1) * P])
                pe.wait_ge(mrg_att, l + 1)
                for q in range(3):
                    rows_slab(m + 1 + q, q, KD, tr + TR_RET + q)
                pe.wait_ge(tr_done, tr + TR_RET + 4)
                slab_ready(m + 4)
                last_rows(lambda t, i: xt(t, 6 + i), m + 4, 0)
                for s in range(4):
                    pe.wait_ge(mrg_ready, 2 * l + s // 2 + 1)
                    turn(tr + TR_MIX + s, [nat[:, t, GA + (2 * s + kk) * P:GA + (2 * s + kk + 1) * P]
                                           for kk in range(2) for t in range(TILES)])
                for q in range(3):
                    rows_slab(m + 5 + q, q, KD, tr + TR_MIX + q)
                pe.wait_ge(tr_done, tr + TR_MIX + 4)
                slab_ready(m + 8)
                last_rows(lambda t, i: xt(t, 6 + i), m + 8, 0)
                pe.wait_ge(xn_ready, 2 * TILES * l + 2 * TILES)
                for s in range(4):
                    turn(tr + TR_H2 + s, [h_nat[:, t, (2 * s + kk) * P:(2 * s + kk + 1) * P]
                                          for kk in range(2) for t in range(TILES)],
                         read=8 * l + 4 + s - 1 if s >= 2 else None)
                    if l == LAYERS - 1 and s:
                        logits_of(s - 1)
                if l == LAYERS - 1:
                    logits_of(3)
                if l == 0:
                    def dense_ready(k):
                        if k < 2:
                            pe.wait_ge(tr_done, tr + TR_H2 + 2 * k + 2)
                        if k - 3 in MOD_AFTER_FFN:
                            m, i = MOD_AFTER_FFN[k - 3]
                            pe.wait_ge(mod_done, 2 * m + i + 1)
                        slab_ready(FFN_M + k)

                    def sum_under(k, q):
                        if k in MOD_AFTER_FFN:
                            mod_sum(*MOD_AFTER_FFN[k], bank[q % 2][:, :, 256:512])

                    ffn(TILES, FFN_M, dense_ready, 0, xt, sum_under=sum_under)

            pe.wait_ge(tr_done, 2 * TR_LAYER)
            for s in range(4):
                if s >= 2:
                    pe.wait_ge(home_done, s - 1)
                for i, (kk, t) in enumerate((kk, t) for kk in range(2) for t in range(TILES)):
                    ins = pe.transpose(ps(6 + s % 2)[:, i * P:(i + 1) * P], hT[:, 2 * s + kk, t * P:(t + 1) * P], ident)
                ins.then_inc(home_psum, 1)
            pe.wait_ge(route_ready, 1)
            member = [route[:, t, 0, 0:EXPERTS] for t in range(TILES)]
            pe.matmul(ps(0)[:, 0:EXPERTS], earlier, member[0], start=True, stop=True)
            pe.matmul(ps(1)[:, 0:EXPERTS], ones, member[0], start=True, stop=False)
            pe.matmul(ps(1)[:, 0:EXPERTS], earlier, member[1], start=False, stop=True)
            pe.matmul(ps(2)[0:1, 0:EXPERTS], ones[:, 0:1], member[0], start=True, stop=False)
            pe.matmul(ps(2)[0:1, 0:EXPERTS], ones[:, 0:1], member[1], start=False, stop=True).then_inc(rank_psum, 1)

            def gather():
                for i in range(2):
                    for kk in range(4):
                        k = 4 * i + kk
                        for t in range(TILES):
                            ins = pe.matmul(ps(2 + i)[:, kk * P:(kk + 1) * P], h_nat[:, t, k * P:(k + 1) * P],
                                            pick[:, t, :], start=(t == 0), stop=(t == 1))
                    ins.then_inc(xg_psum, 1)

            def back(i):
                t, half = divmod(i, 2)
                pe.matmul(ps(6 + i % 2), pickT[:, t * P:(t + 1) * P], y_one[:, half * 512:(half + 1) * 512],
                          start=True, stop=True).then_inc(back_psum, 1)

            pe.wait_ge(routed, 1)
            pe.wait_ge(home_done, 4)
            pe.wait_ge(pick_ready, 2)
            gather()

            with pe.Fori(0, EXPERTS) as e:
                n0 = pe.snap(e * PASS + N_STATIC)
                group0 = pe.snap(e * GF + GF)
                count = pe.value_load(counts[0:1, bass.ds(e, 1)], min_val=0, max_val=T)

                def ready(k):
                    if k == 0:
                        pe.wait_ge(xg_ready, e * 2 + 2)
                    if k == 4:
                        pe.wait_ge(y_ready, e * 3 + 3)
                    pe.wait_ge(lo_done, n0 + (k + 1))

                def after(k):
                    if k == 1:
                        pe.wait_ge(y_ready, e * 3 + 3)
                        back(0)
                        back(1)
                    if k == 2:
                        pe.wait_ge(y_added, e * 4 + 6)
                        back(2)
                        back(3)
                    if k == 6:
                        pe.wait_ge(y_added, e * 4 + 8)
                        for t in range(TILES):
                            pe.transpose(ps(7)[:, t * P:(t + 1) * P], pick[:, t, :], ident)
                        for t in range(TILES):
                            ins = pe.matmul(ps(7)[:, T:T + 1], pick[:, t, :], route_e[:, t, 2:3], start=(t == 0), stop=(t == 1))
                        ins.then_inc(pkT_psum, 1)
                    if k == PASS - 2:
                        pe.wait_ge(pick_ready, e * 2 + 4)
                        gather()

                with pe.If(count > P):
                    def dense_after(k):
                        after({3: 6, 6: -1}.get(k, k))

                    def dense_ready(k):
                        if k == 4:
                            pe.wait_ge(pkT_ready, e + 1)
                            pe.wait_ge(sw_ready, e + 1)
                        ready(k)

                    ffn(TILES, M_STATIC, dense_ready, group0, xt, dense_after)
                with pe.Else():
                    ffn(1, M_STATIC, ready, group0, lambda t, k: (xg_hi[:, k, :], xg_lo[:, k, :]), after)

            pe.wait_ge(y_ready, EXPERTS * 3 + 3)
            for i in range(4):
                if i == 2:
                    pe.wait_ge(y_added, EXPERTS * 4 + 6)
                back(i)

        @block.vector
        def _(dve):
            steps, gone, highs = [0], [0], [0]

            def link(ins):
                steps[0] += 1
                ins.then_inc(dve_step, 1)
                dve.wait_ge(dve_step, steps[0])

            def low(j, at):
                a = at % SPLIT_SLOTS
                dve.tensor_tensor(w_lo[:, a, :], raw(j), w_hi[:, a, :].bitcast(F32), ALU.subtract).then_inc(lo_done, 1)

            def accumulate(n):
                _, l, a, q = SLABS[n]
                m = CHUNK_AT[(l, a)]
                dve.wait_ge(slab_in[SLOT[n]], 16 * USE[n])
                if q == 0:
                    dve.wait_ge(c_ready, 1)
                    if m == 0:
                        dve.wait_ge(first_bias, 32)
                    else:
                        dve.wait_ge(in_bias[m % 2], 32 * ((m + 1) // 2))
                for i in range(2):
                    k = 2 * q + i
                    ins = dve.scalar_tensor_tensor(acc(m), raw(SLOT[n])[:, i * D:(i + 1) * D], c_act[:, k:k + 1], acc(m),
                                                   ALU.mult, ALU.add)
                    if i == 0:
                        link(ins)
                ins.then_inc(lo_done, 1)
                dve.wait_ge(lo_done, n + 1)
                if q == 3:
                    dve.sem_inc(acc_ready, 1)

            def ahead(m):
                while gone[0] <= PRODUCTS[min(m, M_STATIC - 1)]:
                    n = gone[0]
                    if SLABS[n][0] == "ada":
                        accumulate(n)
                    else:
                        dve.wait_ge(hi_done, NUMBER[n] + 1)
                        low(SLOT[n], NUMBER[n])
                    gone[0] += 1

            def tr_low(step, hi, lo, src):
                dve.wait_ge(tr_hi, highs[0] + 1)
                highs[0] += 1
                dve.tensor_tensor(lo, src, hi.bitcast(F32), ALU.subtract).then_inc(tr_done, 1)

            def variance(k, t):
                dve.wait_ge(ss_ready, TILES * k + t + 1)
                dve.tensor_scalar(var[:, t:t + 1], ssum[:, t:t + 1], 1.0 / D, EPS, ALU.mult, ALU.add).then_inc(var_ready, 1)
                dve.wait_ge(std_ready, TILES * k + t + 1)
                link(dve.reciprocal(rstd[:, t:t + 1], std[:, t:t + 1]))

            def modulated(which, step0, keep, first=0, end=4):
                dst = [h_tmp[:, s % 2, :, :] if keep is None else keep[:, 2 * s:2 * s + 2, :] for s in range(4)]

                def lower(s):
                    tr_low(step0 + s, xt_hi[:, 2 * s:2 * s + 2, :], xt_lo[:, 2 * s:2 * s + 2, :], dst[s])

                for s in range(first, end):
                    step = step0 + s
                    dve.wait_ge(tr_psum, step + 1)
                    if keep is None and s >= 2:
                        dve.wait_ge(tr_done, step - 1)
                    for i in range(2):
                        k = 2 * s + i
                        ins = dve.tensor_scalar(dst[s][:, i, :], ps(turn_bank(step))[:, i * T:(i + 1) * T],
                                                scale[:, which, k:k + 1], shift[:, which, k:k + 1], ALU.mult, ALU.add)
                    ins.then_inc(tr_mod, 1)
                    if s > first:
                        lower(s - 1)
                lower(end - 1)

            def plain(step0, steps_n):
                for s in range(steps_n):
                    src = ps(turn_bank(step0 + s)).rearrange("p (c n) -> p c n", c=2)
                    tr_low(step0 + s, xt_hi[:, 2 * s:2 * s + 2, :], xt_lo[:, 2 * s:2 * s + 2, :], src)

            def mod_in(m, i, at=None):
                l, a = CHUNKS[m]
                j = 2 * l + a // 3
                if a % 3 == 2:
                    dve.wait_ge(mod_psum, m + 1)
                    dve.wait_ge(in_gain[a // 3], 16 * (l + 1))
                    dve.tensor_tensor(G[:, a // 3, :], pair(3), G[:, a // 3, :], ALU.mult).then_inc(mod_done, 2)
                    return
                at = whole(7) if at is None else at
                dve.wait_ge(mod_turned, COLUMN_HALVES[m] + i + 1)
                n = KD // 2
                ks = slice(a % 3 * n, (a % 3 + 1) * n)
                dst = (shift, scale)[i][:, j, ks]
                ins = dve.tensor_reduce(dst.rearrange("p (t b) -> p t b", t=TILES),
                                        at.rearrange("p t (b n) -> p t b n", b=2), AX, ALU.add)
                if i:
                    link(ins)
                    ins = dve.scalar_tensor_tensor(dst, dst, 1.0, gains[:, j, ks], ALU.add, ALU.mult)
                ins.then_inc(mod_done, 1)

            def add_norm(k, l, which, srcs, tmp):
                for t in range(TILES):
                    variance(k, t)
                    if t:
                        dve.wait_ge(x_done, 2 * TILES * l + TILES * which + t)
                    link(dve.scalar_tensor_tensor(tmp, srcs[t], rstd[:, t:t + 1], G[:, which, :], ALU.mult, ALU.mult))
                    dve.tensor_tensor(X[:, t, :], X[:, t, :], tmp, ALU.add).then_inc(x_done, 1)
                dve.wait_ge(x_done, 2 * TILES * l + TILES * (which + 1))

            def normed(k, dst):
                for t in range(TILES):
                    variance(k, t)
                    dve.tensor_scalar(dst[:, t, :], X[:, t, :], rstd[:, t:t + 1], None, ALU.mult).then_inc(xn_ready, 1)

            def ffn_task(k, tiles, group0):
                kind, g, h = FFN_ORDER[k]
                if (kind, h) == ("gu", 1):
                    dve.wait_ge(s_ready, group0 + (g + 1))
                    if not (isinstance(group0, int) and group0 + g == 0):
                        dve.wait_ge(aT_psum, group0 + g)
                    v = bank[g % 2][:, 0:tiles, 256:512]
                    dve.tensor_tensor(act_m[:, 0:tiles, :], act_s[:, 0:tiles, :], v, ALU.mult).then_inc(a_ready, 1)
                if ((kind, h) == ("gu", 0) and g > 0) or (kind, g) == ("dn", GF - 2):
                    q = g - 1 if kind == "gu" else GF - 1
                    dve.wait_ge(aT_hi_ready, group0 + (q + 1))
                    v = bank[q % 2][:, 0:tiles, 0:256]
                    dve.tensor_tensor(aT_lo[:, 0:tiles, :], v, aT_hi[:, 0:tiles, :].bitcast(F32), ALU.subtract)\
                       .then_inc(aT_ready, 1)

            def expert_split(k, m0):
                dve.wait_ge(hi_done, m0 + (k + 1))
                low(k % FFN_SLOTS, M_STATIC + k)

            norm = 0
            for l in range(LAYERS):
                tr = TR_LAYER * l
                if l == 0:
                    while SLABS[gone[0]][0] == "ada":
                        if gone[0] == 3:
                            normed(norm, xn_mix); norm += 1
                        accumulate(gone[0])
                        gone[0] += 1
                    ahead(WIN_M[l])
                    for i in range(2):
                        mod_in(0, i, whole(4 + i))
                    dve.wait_ge(mod_done, 2)
                    modulated(0, tr + TR_H, None, 0, 2)
                    ahead(WIN_M[l] + 1)
                else:
                    normed(norm, xn_mix); norm += 1
                    dve.wait_ge(mod_done, 20)
                    modulated(2 * l, tr + TR_H, None)

                def win_out(s):
                    if s not in WIN_OUT:
                        return
                    g = WIN_OUT[s]
                    dve.wait_ge(pe_done, WIN_M[l] + s + 1)
                    src = bank[g % 2][:, 1, :]
                    if g < QK_GROUPS:
                        cb = 4 * g + 2
                        dst = qkT[:, cb:cb + 2, :].rearrange("p c n -> p (c n)")
                        dve.tensor_scalar(dst, src, DH ** -0.5 if cb < 6 else 1.0, None, ALU.mult).then_inc(ev_dve, 1)
                    else:
                        at = (g - QK_GROUPS) * 512
                        w = min(512, NAT_COLS - at)
                        dve.tensor_copy(nat[:, 1, at:at + w], src[:, 0:w]).then_inc(ev_dve, 1)

                def attention(i):
                    h = HEADS * l + i
                    if i < HEADS:
                        g, hh = divmod(i, HG)
                        dve.wait_ge(sc_psum, h + 1)
                        if h >= 2:
                            dve.wait_ge(pT_psum, h - 1)
                        if i < 2 and l:
                            dve.wait_ge(ro_psum, RH // 2 * l)
                        o = ps(4)
                        pr = probs[:, i % 2, :]
                        dve.scalar_tensor_tensor(pr[:, 0:P], dist[:, g, P:2 * P], -SLOPES[i], o[:, 0:P], ALU.mult, ALU.add)
                        link(dve.scalar_tensor_tensor(pr[:, P:3 * P], dist[:, g, :], -SLOPES[i], o[:, P:3 * P],
                                                      ALU.mult, ALU.add))
                        link(dve.tensor_reduce(neg_max[:, g, hh, 0:1], pr[:, 0:P], AX, ALU.max, negate=True))
                        dve.tensor_reduce(neg_max[:, g, hh, 1:2], pr[:, P:3 * P], AX, ALU.max, negate=True)\
                           .then_inc(sm_ready, 1)
                    j = i - 2
                    if j >= 0 and j % HG == HG - 1:
                        dve.wait_ge(pv_psum, HEADS * l + j + 1)
                        dve.tensor_copy(og[:, j // HG, :, :].rearrange("p t n -> p (t n)"), ps(6)).then_inc(og_done, 1)

                def group_weights(part):
                    if part == 0:
                        dve.wait_ge(ln_ready, l + 1)
                        dve.wait_ge(sm_ready, HEADS * (l + 1))
                        link(dve.tensor_tensor(lse[:, :, :, :], lse[:, :, :, :], neg_max[:, :, :, :], ALU.subtract))
                        link(dve.tensor_tensor(top[:, :, :], lse[:, 0, :, :], lse[:, 1, :, :], ALU.max))
                        link(dve.tensor_tensor(top[:, :, :], top[:, :, :], lse[:, 2, :, :], ALU.max))
                        for g in range(GROUPS):
                            ins = dve.tensor_tensor(lse[:, g, :, :], lse[:, g, :, :], top[:, :, :], ALU.subtract)
                            ins.then_inc(lse_ready, 1) if g == GROUPS - 1 else link(ins)
                        link(dve.reciprocal(den[:, :, :, :], den[:, :, :, :]))
                    if part == 1:
                        dve.wait_ge(ex_ready, l + 1)
                        link(dve.tensor_tensor(top[:, :, :], coef[:, 0, :, :], coef[:, 1, :, :], ALU.add))
                        link(dve.tensor_tensor(top[:, :, :], top[:, :, :], coef[:, 2, :, :], ALU.add))
                        link(dve.reciprocal(top[:, :, :], top[:, :, :]))
                        link(dve.tensor_tensor(coef[:, :, :, :], coef[:, :, :, :], den[:, :, :, :], ALU.mult))
                        for g in range(GROUPS):
                            ins = dve.tensor_tensor(coef[:, g, :, :], coef[:, g, :, :], top[:, :, :], ALU.mult)
                            if g == GROUPS - 1:
                                link(ins)
                    if part == 2:
                        dve.wait_ge(og_done, GROUPS * (l + 1))
                        for g in range(GROUPS):
                            for t in range(TILES):
                                v = og[:, g, t, :].rearrange("p (h n) -> p h n", h=HG)
                                w = coef[:, g, :, t:t + 1].to_broadcast([P, HG, DH])
                                ins = dve.tensor_tensor(v, v, w, ALU.mult)
                        link(ins)
                        link(dve.tensor_tensor(og[:, 0, :, :], og[:, 0, :, :], og[:, 1, :, :], ALU.add))
                        dve.tensor_tensor(og[:, 0, :, :], og[:, 0, :, :], og[:, 2, :, :], ALU.add).then_inc(att_ready, 1)

                def retention(p):
                    if 1 <= p <= RH // 2:
                        dve.wait_ge(ro_psum, RH // 2 * l + p)
                        j = 2 * (p - 1)
                        dst = nat[:, :, QR + j * RDV:QR + (j + 2) * RDV].rearrange("p t (h n) -> p t h n", h=2)
                        dve.tensor_copy(dst, ps(6).rearrange("p (h t n) -> p t h n", h=2, t=TILES)).then_inc(ro_done, 1)
                    if p < RH // 2:
                        for i in head_pair(p):
                            r = RH * l + i
                            dve.wait_ge(rs_psum, r + 1)
                            dve.wait_ge(dec_ready, r + 1)
                            if i < 2:
                                dve.wait_ge(pT_psum, HEADS * (l + 1))
                            o = ps(4 + i % 2)
                            pr = probs[:, i % 2, :]
                            dve.tensor_tensor(pr[:, 0:T], o[:, 0:T], decay[:, i % 2, :], ALU.mult).then_inc(dve_step, 1)
                            steps[0] += 1
                            dve.tensor_tensor(pr[:, T:T + P], o[:, T:T + P], decay[:, i % 2, 0:P], ALU.mult).then_inc(rp_ready, 1)
                    if p >= 2:
                        q = p - 2
                        dve.wait_ge(sq_ready, RH // 2 * l + q + 1)
                        v = sq[:, :, 2 * q * RDV:2 * (q + 1) * RDV].rearrange("p t (h n) -> p t h n", h=2)
                        dve.tensor_reduce(r_sum[:, :, 2 * q:2 * q + 2], v, AX, ALU.add).then_inc(dve_step, 1)
                        steps[0] += 1

                for s in range(WIN_SLABS):
                    if l == 0 and s == 1:
                        for i in range(2):
                            mod_in(1, i, whole(4 + i))
                        dve.wait_ge(mod_done, 4)
                        modulated(0, tr + TR_H, None, 2, 4)
                    ahead(WIN_M[l] + s + 2)
                    win_out(s)
                    if s in MOD_AFTER_WIN[l]:
                        mod_in(*MOD_AFTER_WIN[l][s])
                    if s == ATT_FROM:
                        dve.wait_ge(in_table, 16 * (l + 1))
                    if ATT_FROM <= s < ATT_FROM + HEADS + 2:
                        attention(s - ATT_FROM)
                    if TURN_FROM <= s < TURN_FROM + 4:
                        i = s - TURN_FROM
                        dst, at = ((qrT, 2 * i) if i < 2 else (krT, 2 * i - 4))
                        step = tr + TR_RQ + i
                        dve.wait_ge(tr_psum, step + 1)
                        dve.tensor_scalar(dst[:, at:at + 2, :].rearrange("p c n -> p (c n)"), ps(7),
                                          1.0 if i < 2 else RDK ** -0.5, None, ALU.mult).then_inc(tr_done, 1)
                    if s >= RET_FROM:
                        retention(s - RET_FROM)
                        if s - RET_FROM < 3:
                            group_weights(s - RET_FROM)
                    if s == ATT_TURN:
                        tr_low(tr + TR_ATT, att_hi, att_lo, ps(turn_bank(tr + TR_ATT)).rearrange("p (c n) -> p c n", c=2))
                retention(RH // 2 + 1)
                dve.wait_ge(dve_step, steps[0])
                dve.tensor_scalar(r_var[:, :, :], r_sum[:, :, :], 1.0 / RDV, EPS, ALU.mult, ALU.add).then_inc(r_var_ready, 1)
                dve.wait_ge(r_std_ready, l + 1)
                dve.reciprocal(r_sum[:, :, :], r_std[:, :, :]).then_inc(r_rstd_ready, 1)
                dve.wait_ge(r_rstd_ready, l + 1)
                dve.wait_ge(gated, RH // 2 * (l + 1))
                for h in range(RH):
                    v = nat[:, 1, QR + h * RDV:QR + (h + 1) * RDV]
                    ins = dve.tensor_scalar(v, v, r_sum[:, 1, h:h + 1], None, ALU.mult)
                ins.then_inc(ret_ready, 1)
                m = ATT_M[l]
                dve.wait_ge(pe_done, m + 1)
                dve.wait_ge(gates_ready, TILES * (2 * l + 1))
                for t in range(TILES):
                    v = nat[:, t, GA:GA + D]
                    ins = dve.tensor_tensor(v, v, pair(t), ALU.mult)
                ins.then_inc(mrg_att, 1)
                plain(tr + TR_RET, 4)
                ahead(m + 5)
                dve.wait_ge(mrg_att, l + 1)
                dve.wait_ge(gates_ready, TILES * (2 * l + 2))
                dve.wait_ge(tile_done, 3 * l + 1)
                v, w = nat[:, :, GA:GA + D], nat[:, :, GB:GB + D]
                link(dve.tensor_tensor(w[:, 0, :], w[:, 0, :], pair(0), ALU.mult))
                dve.tensor_tensor(v[:, 0, :], v[:, 0, :], w[:, 0, :], ALU.add)
                dve.wait_ge(pe_done, m + 5)
                for half in range(2):
                    c = slice(half * 512, (half + 1) * 512)
                    link(dve.tensor_tensor(w[:, 1, c], w[:, 1, c], ps(2 + half), ALU.mult))
                    dve.tensor_tensor(v[:, 1, c], v[:, 1, c], w[:, 1, c], ALU.add).then_inc(mrg_ready, 1)
                plain(tr + TR_MIX, 4)
                ahead(m + 9)
                if l == LAYERS - 1:
                    expert_split(0, M_STATIC)
                add_norm(norm, l, 0, [pair(t) for t in range(TILES)], scratch); norm += 1
                normed(norm, h_nat); norm += 1
                if l == LAYERS - 1:
                    modulated(2 * l + 1, tr + TR_H2, hT)
                else:
                    modulated(2 * l + 1, tr + TR_H2, None)
                    for k in range(PASS):
                        ahead(FFN_M + min(k + 2, PASS))
                        ffn_task(k, TILES, 0)
                        if k in MOD_AFTER_FFN:
                            g = FFN_ORDER[k][1]
                            q = g - 1 if k < PASS - 2 else GF - 1
                            mod_in(*MOD_AFTER_FFN[k], bank[q % 2][:, :, 256:512])
                    add_norm(norm, l, 1, [pair(2 + t) for t in range(TILES)], h_nat[:, 0, :]); norm += 1

            for t in range(TILES):
                dve.wait_ge(lg_psum, 1)
                link(dve.tensor_tensor(logits[:, t, :], ps(4 + t)[:, 0:EXPERTS], router_b[:, :], ALU.add))
                link(dve.max(best[:, t, :], logits[:, t, :]))
                link(dve.max_index(best_i[:, t, :], best[:, t, :], logits[:, t, :]))
            link(dve.memset(route[:, :, :, :], 0.0))
            link(dve.tensor_copy(best_f[:, :, :], best_i[:, :, :]))
            dve.tensor_tensor(gate[:, :, 0], best[:, :, 1], best[:, :, 0], ALU.subtract).then_inc(bd_ready, 1)
            for t in range(TILES):
                for j in range(2):
                    link(dve.tensor_scalar(one_hot[:, t, j, :], iota[:, 0:EXPERTS], best_f[:, t, j:j + 1], None, ALU.is_equal))
            for t in range(TILES):
                ins = dve.tensor_tensor(route[:, t, 0, 0:EXPERTS], one_hot[:, t, 0, :], one_hot[:, t, 1, :], ALU.add)
                ins.then_inc(route_ready, 1) if t == TILES - 1 else link(ins)
            dve.wait_ge(e2_ready, 1)
            link(dve.tensor_scalar(gate[:, :, 0], gate[:, :, 1], 1.0, None, ALU.add))
            link(dve.reciprocal(gate[:, :, 0], gate[:, :, 0]))
            link(dve.tensor_tensor(gate[:, :, 1], gate[:, :, 1], gate[:, :, 0], ALU.mult))
            for t in range(TILES):
                w = route[:, t, 2, 0:EXPERTS]
                link(dve.tensor_scalar(w, one_hot[:, t, 0, :], gate[:, t, 0:1], None, ALU.mult))
                link(dve.scalar_tensor_tensor(w, one_hot[:, t, 1, :], gate[:, t, 1:2], w, ALU.mult, ALU.add))
            dve.wait_ge(rank_psum, 1)
            for t in range(TILES):
                link(dve.tensor_copy(route[:, t, 1, 0:EXPERTS], ps(t)[:, 0:EXPERTS]))
            dve.tensor_copy(counts[0:1, :], ps(2)[0:1, 0:EXPERTS]).then_inc(routed, 1)
            dve.wait_ge(routed, 1)

            def pick_expert(e, value):
                dve.tensor_copy(route_e[:, :, :].rearrange("p t a -> p (t a)"),
                                route[:, :, :, bass.ds(e, 1)].rearrange("p t a e -> p (t a e)")).then_inc(col_ready, 1)
                dve.wait_ge(col_ready, value + 1)
                for t in range(TILES):
                    dve.tensor_scalar(pick[:, t, :], iota, route_e[:, t, 1:2], route_e[:, t, 0:1],
                                      ALU.is_equal, ALU.mult).then_inc(pick_ready, 1)

            def gathered_low(value):
                for i in range(2):
                    dve.wait_ge(xg_hi_ready, value + (i + 1))
                    hi, lo = (b[:, 4 * i:4 * i + 4, :].rearrange("p k n -> p (k n)") for b in (xg_hi, xg_lo))
                    dve.tensor_tensor(lo, ps(2 + i), hi.bitcast(F32), ALU.subtract).then_inc(xg_ready, 1)

            pick_expert(0, 0)
            dve.wait_ge(home_psum, 4)
            dve.memset(y_sum[:, :, :], 0.0).then_inc(y_added, 4)
            dve.wait_ge(y_added, 4)
            dve.memset(y_one, 0.0).then_inc(y_ready, 1)
            dve.memset(pickT[:, :], 0.0).then_inc(y_ready, 2)
            expert_split(1, M_STATIC)
            gathered_low(0)

            with dve.Fori(0, EXPERTS) as e:
                m0 = dve.snap(e * PASS + M_STATIC)
                group0 = dve.snap(e * GF + GF)
                e1 = dve.snap(e + 1)
                count = dve.value_load(counts[0:1, bass.ds(e, 1)], min_val=0, max_val=T)

                def add_back(i):
                    t, half = divmod(i, 2)
                    dve.wait_ge(back_psum, e * 4 + (i + 1))
                    y = y_sum[:, t, half * 512:(half + 1) * 512]
                    dve.tensor_tensor(y, y, ps(6 + i % 2), ALU.add).then_inc(y_added, 1)

                def expert(tiles):
                    turned = 3 if tiles == TILES else 6
                    for k in range(PASS):
                        expert_split(k + 2, m0)
                        ffn_task(k, tiles, group0)
                        if k in (1, 2):
                            add_back(2 * k - 2)
                            add_back(2 * k - 1)
                        if k == turned:
                            dve.wait_ge(pkT_ready, e + 1)
                            dve.tensor_copy(slot_w[:, :], ps(7)[:, T:T + 1]).then_inc(sw_ready, 1)
                        if k == 12:
                            pick_expert(e1, e1)
                        if k == PASS - 2:
                            gathered_low(e * 2 + 2)

                with dve.If(count > P):
                    dve.wait_ge(y_ready, e * 3 + 3)
                    dve.tensor_copy(all_w[:, :], route[:, :, 2, bass.ds(e, 1)].rearrange("p t e -> p (t e)"))\
                       .then_inc(allw_ready, 1)
                    expert(TILES)
                    dve.wait_ge(pe_done, m0 + PASS)
                    dve.wait_ge(allw_ready, e + 1)
                    for t in range(TILES):
                        dve.scalar_tensor_tensor(y_sum[:, t, :], pair(2 + t), all_w[:, t:t + 1], y_sum[:, t, :],
                                                 ALU.mult, ALU.add).then_inc(y_ready, 1)
                    dve.memset(y_one, 0.0).then_inc(y_ready, 1)
                with dve.Else():
                    dve.sem_inc(allw_ready, 1)
                    expert(1)

            for i in range(4):
                t, half = divmod(i, 2)
                dve.wait_ge(back_psum, EXPERTS * 4 + i + 1)
                y = y_sum[:, t, half * 512:(half + 1) * 512]
                dve.tensor_tensor(y, y, ps(6 + i % 2), ALU.add).then_inc(y_added, 1)
            add_norm(norm, LAYERS - 1, 1, [y_sum[:, t, :] for t in range(TILES)], h_nat[:, 0, :])


def kernel(**inputs):
    import numpy as _np
    import concourse.bacc as _bacc
    from concourse import mybir as _mybir
    from concourse.bass_utils import run_bass_kernel_spmd as _run

    mix_table, perm_table = host_constants()
    a = {k: _np.ascontiguousarray(v) for k, v in inputs.items()}
    cols = lambda v: v.reshape(-1, KD, P).transpose(2, 0, 1).reshape(P, -1)
    gain_cols = _np.stack([a["norm_pre_mix"], a["norm_pre_ffn"]], 1)
    stream, experts = lay_out_weights(a)
    laid = [
        ("x", a["x"]), ("c_cols", cols(a["c"])), ("b_ada", a["b_ada"]), ("stream", stream), ("experts", experts),
        ("gain_cols", cols(gain_cols)), ("post_mix", a["norm_post_mix"]), ("post_ffn", a["norm_post_ffn"]),
        ("w_router", a["w_router"]), ("b_router", a["b_router"]), ("mix_table", mix_table), ("perm_table", perm_table),
    ]
    nc = _bacc.Bacc("TRN2", target_bir_lowering=False, num_devices=1)
    arrays, args = {}, []
    for name, v in laid:
        v = _np.ascontiguousarray(v)
        arrays[f"in_{name}_dram"] = v
        args.append(nc.dram_tensor(f"in_{name}_dram", v.shape, _mybir.dt.from_np(v.dtype), kind="ExternalInput").ap())
    out = nc.dram_tensor("out_0_dram", (1, T, D), F32, kind="ExternalOutput").ap()
    hybrid_block_kernel(nc, *args, out)
    r = _run(nc, [arrays], core_ids=[0])
    return r.results[0]["out_0_dram"]
```
